# Optimizing a Trainium2 kernel written in Bass

```python
import math
import jax
import jax.numpy as jnp
from jax import lax
import numpy as np

D_MODEL = 1024
BATCH = 1
SEQ = 1024
DEPTH = 2

GRID_W = 64
CTX_LEN = 256
ROPE_BASE = 10000.0

A_HEADS = 4
A_DQK = D_MODEL // (8 * A_HEADS)
A_DV = 2 * A_DQK
A_WIDTH = A_HEADS * A_DV
A_QK = A_HEADS * 2 * A_DQK
Q_BLOCK = 128

B_HEADS = 4
B_DK = D_MODEL // (4 * B_HEADS)
B_DV = D_MODEL // (4 * B_HEADS)
B_WIDTH = B_HEADS * B_DV
B_QK = B_HEADS * B_DK
RET_CHUNK = 128
RET_LOG_GAMMA = tuple(math.log(1.0 - 2.0 ** (-5 - h)) for h in range(B_HEADS))

C_GROUPS = 4
C_WIDTH = D_MODEL // 4
C_GW = C_WIDTH // C_GROUPS
POOL_WINDOWS = (2, 4, 8, 16)

D_WIDTH = D_MODEL // 4
CONV_K = 31

MIX_WIDTH = A_WIDTH + B_WIDTH + C_WIDTH + D_WIDTH
D_FF = ((8 * D_MODEL + 3 * 256 - 1) // (3 * 256)) * 256

COL_SIZES = (A_QK, A_WIDTH, B_QK, B_WIDTH, A_QK, B_QK, B_WIDTH, B_WIDTH, C_WIDTH, 2 * D_WIDTH)
CTX_COLS = A_QK + A_WIDTH + B_QK + B_WIDTH
IN_COLS = sum(COL_SIZES)

kernel_name = 'hybrid_diffusion_parallel_groups'

def _rms_norm(x, g, eps=1e-6):
    xf = x.astype(jnp.float32)
    y = xf * lax.rsqrt(jnp.mean(xf * xf, axis=-1, keepdims=True) + eps)
    return (y * g.astype(jnp.float32)).astype(x.dtype)

def _layer_norm(x, g, b, eps=1e-5):
    xf = x.astype(jnp.float32)
    mu = jnp.mean(xf, axis=-1, keepdims=True)
    var = jnp.mean(jnp.square(xf - mu), axis=-1, keepdims=True)
    y = (xf - mu) * lax.rsqrt(var + eps) * g.astype(jnp.float32) + b.astype(jnp.float32)
    return y.astype(x.dtype)

def _modulate(h, shift, scale):
    return h * (1 + scale) + shift

def _split_cols(u):
    parts, start = [], 0
    for size in COL_SIZES:
        if start >= u.shape[-1]:
            break
        parts.append(u[..., start:start + size])
        start += size
    return parts

def _axial_rope(row, col, d, dtype):
    n_freq = d // 4
    inv = ROPE_BASE ** (-jnp.arange(n_freq, dtype=jnp.float32) / n_freq)
    ang = jnp.concatenate([row.astype(jnp.float32)[:, None] * inv,
                           col.astype(jnp.float32)[:, None] * inv], axis=-1)
    return jnp.cos(ang).astype(dtype), jnp.sin(ang).astype(dtype)

def _apply_rope(x, cos, sin):
    x1, x2 = jnp.split(x, 2, axis=-1)
    return jnp.concatenate([x1 * cos - x2 * sin, x1 * sin + x2 * cos], axis=-1)

def _heads_qk(u):
    b, t, _ = u.shape
    return u.reshape(b, t, A_HEADS, 2, A_DQK).transpose(0, 2, 3, 1, 4)

def _heads_v(u, n_heads):
    b, t, w = u.shape
    return u.reshape(b, t, n_heads, w // n_heads).transpose(0, 2, 1, 3)

def _diff_attend(q, k, v, lam):
    s = jnp.einsum('bhcqd,bhckd->bhcqk', q, k, preferred_element_type=jnp.float32) * (A_DQK ** -0.5)
    p = jax.nn.softmax(s, axis=-1)
    w = p[:, :, 0] - lam * p[:, :, 1]
    return jnp.einsum('bhqk,bhkd->bhqd', w.astype(v.dtype), v)

def _diff_attn_blocks(q, k_all, v_all, lam):
    b, h, _, t, d = q.shape
    nb = t // Q_BLOCK
    qb = q.reshape(b, h, 2, nb, Q_BLOCK, d).transpose(3, 0, 1, 2, 4, 5)
    out = lax.map(lambda qi: _diff_attend(qi, k_all, v_all, lam), qb)
    return out.transpose(1, 2, 0, 3, 4).reshape(b, h, t, A_DV)

def _diff_head_out(o, g, lam_init):
    b, h, t, dv = o.shape
    o = _rms_norm(o.transpose(0, 2, 1, 3), g, eps=1e-5) * (1.0 - lam_init)
    return o.reshape(b, t, h * dv)

def _chunk(x):
    b, h, t, d = x.shape
    return x.reshape(b, h, t // RET_CHUNK, RET_CHUNK, d)

def _ret_scan(kc, vc, s0):
    c = kc.shape[3]
    lg = jnp.asarray(RET_LOG_GAMMA, jnp.float32)
    j = jnp.arange(c, dtype=jnp.float32)
    w_end = jnp.exp(lg[:, None] * (c - 1.0 - j))
    kv = jnp.einsum('bhncd,hc,bhnce->nbhde', kc.astype(jnp.float32), w_end,
                    vc.astype(jnp.float32))
    chunk_decay = jnp.exp(lg * c)[None, :, None, None]

    def step(s, kv_n):
        return chunk_decay * s + kv_n, s

    s_fin, s_prev = lax.scan(step, s0, kv)
    return s_prev, s_fin

def _ret_out(qc, kc, vc, s_prev):
    c = qc.shape[3]
    lg = jnp.asarray(RET_LOG_GAMMA, jnp.float32)
    j = jnp.arange(c, dtype=jnp.float32)
    dist = j[:, None] - j[None, :]
    dmat = jnp.where(dist >= 0, jnp.exp(lg[:, None, None] * jnp.maximum(dist, 0.0)), 0.0)
    qf, kf, vf = qc.astype(jnp.float32), kc.astype(jnp.float32), vc.astype(jnp.float32)
    scores = jnp.einsum('bhncd,bhnmd->bhncm', qf, kf) * dmat[None, :, None]
    y = jnp.einsum('bhncm,bhnme->bhnce', scores, vf)
    cross_decay = jnp.exp(lg[:, None] * (j + 1.0))
    y = y + jnp.einsum('bhncd,nbhde->bhnce', qf, s_prev) * cross_decay[None, :, None, :, None]
    b, h, n, _, dv = y.shape
    return y.reshape(b, h, n * c, dv)

def _retention(q, k, v, s0):
    qc, kc, vc = _chunk(q), _chunk(k), _chunk(v)
    s_prev, s_fin = _ret_scan(kc, vc, s0)
    return _ret_out(qc, kc, vc, s_prev), s_fin

def _head_layer_norm(y, dtype, eps=1e-6):
    b, h, t, d = y.shape
    mu = jnp.mean(y, axis=-1, keepdims=True)
    var = jnp.mean(jnp.square(y - mu), axis=-1, keepdims=True)
    yn = (y - mu) * lax.rsqrt(var + eps)
    return yn.transpose(0, 2, 1, 3).reshape(b, t, h * d).astype(dtype)

def _pool_mixer(u, w_pool_l, s_pool_l):
    b, t, cw = u.shape
    uf = u.astype(jnp.float32)
    csum = jnp.concatenate([jnp.zeros((b, 1, cw), jnp.float32), jnp.cumsum(uf, axis=1)], axis=1)
    pos = jnp.arange(t)
    parts = []
    for g, w in enumerate(POOL_WINDOWS):
        lo = jnp.clip(pos - w // 2, 0, t)
        hi = jnp.clip(pos + w - w // 2, 0, t)
        cs = csum[..., g * C_GW:(g + 1) * C_GW]
        mean = (cs[:, hi] - cs[:, lo]) / (hi - lo).astype(jnp.float32)[None, :, None]
        parts.append(mean - uf[..., g * C_GW:(g + 1) * C_GW])
    d = jnp.stack(parts, axis=2)
    y = jnp.einsum('btgc,gce->btge', d, w_pool_l.astype(jnp.float32)).reshape(b, t, cw)
    return (y * s_pool_l.astype(jnp.float32)).astype(u.dtype)

def _conformer_conv(u, conv_w_l, conv_b_l, ln_g_l, ln_b_l, w_pw2_l):
    a, g = jnp.split(u, 2, axis=-1)
    h = a * jax.nn.sigmoid(g)
    h = lax.conv_general_dilated(h, conv_w_l, window_strides=(1,),
                                 padding=[(CONV_K // 2, CONV_K // 2)],
                                 dimension_numbers=('NWC', 'WIO', 'NWC'),
                                 feature_group_count=D_WIDTH) + conv_b_l
    h = _layer_norm(h, ln_g_l, ln_b_l)
    return jax.nn.silu(h) @ w_pw2_l

def _swiglu(h, wg, wu, wd):
    return (jax.nn.silu(h @ wg) * (h @ wu)) @ wd

def _mixing(u_lat, u_ctx, w_in_l, w_out_l, lam, lam_init, g_subln_l, w_pool_l, s_pool_l,
            conv_w_l, conv_b_l, conv_ln_g_l, conv_ln_b_l, w_conv_out_l, rope_a, rope_b, last):
    dtype = u_lat.dtype
    bsz = u_lat.shape[0]
    p_lat = u_lat @ w_in_l
    p_ctx = u_ctx @ (w_in_l[:, :CTX_COLS] if last else w_in_l)
    kA_l, vA_l, kB_l, vB_l, qA_l, qB_l, gF_l, gB_l, pool_l, glu_l = _split_cols(p_lat)
    pc = _split_cols(p_ctx)

    qA = _apply_rope(_heads_qk(qA_l), *rope_a)
    kA_ctx = _heads_qk(pc[0])
    vA_ctx = _heads_v(pc[1], A_HEADS)
    kA_all = jnp.concatenate([kA_ctx, _apply_rope(_heads_qk(kA_l), *rope_a)], axis=3)
    vA_all = jnp.concatenate([vA_ctx, _heads_v(vA_l, A_HEADS)], axis=2)
    yA_lat = _diff_head_out(_diff_attn_blocks(qA, kA_all, vA_all, lam), g_subln_l, lam_init)

    k_scale = B_DK ** -0.5
    qB = _apply_rope(_heads_v(qB_l, B_HEADS), *rope_b)
    kB = _apply_rope(_heads_v(kB_l, B_HEADS), *rope_b) * k_scale
    vB = _heads_v(vB_l, B_HEADS)
    kB_ctx = _heads_v(pc[2], B_HEADS) * k_scale
    vB_ctx = _heads_v(pc[3], B_HEADS)
    s0 = jnp.zeros((bsz, B_HEADS, B_DK, B_DV), jnp.float32)
    flip = lambda t: jnp.flip(t, axis=2)
    if last:
        s_cf = _ret_scan(_chunk(kB_ctx), _chunk(vB_ctx), s0)[1]
        s_cb = _ret_scan(_chunk(flip(kB_ctx)), _chunk(flip(vB_ctx)), s0)[1]
    else:
        qB_ctx = _heads_v(pc[5], B_HEADS)
        yf_c, s_cf = _retention(qB_ctx, kB_ctx, vB_ctx, s0)
        yb_c, s_cb = _retention(flip(qB_ctx), flip(kB_ctx), flip(vB_ctx), s0)
        yB_ctx = (jax.nn.silu(pc[6]) * _head_layer_norm(yf_c, dtype)
                  + jax.nn.silu(pc[7]) * _head_layer_norm(flip(yb_c), dtype))
    yf = _retention(qB, kB, vB, s_cf)[0]
    yb = flip(_retention(flip(qB), flip(kB), flip(vB), s_cb)[0])
    yB_lat = jax.nn.silu(gF_l) * _head_layer_norm(yf, dtype) + jax.nn.silu(gB_l) * _head_layer_norm(yb, dtype)

    yC_lat = _pool_mixer(pool_l, w_pool_l, s_pool_l)
    yD_lat = _conformer_conv(glu_l, conv_w_l, conv_b_l, conv_ln_g_l, conv_ln_b_l, w_conv_out_l)

    y_lat = jnp.concatenate([yA_lat, yB_lat, yC_lat, yD_lat], axis=-1) @ w_out_l
    if last:
        return y_lat, None
    yA_ctx = _diff_head_out(_diff_attend(_heads_qk(pc[4]), kA_ctx, vA_ctx, lam), g_subln_l, lam_init)
    yC_ctx = _pool_mixer(pc[8], w_pool_l, s_pool_l)
    yD_ctx = _conformer_conv(pc[9], conv_w_l, conv_b_l, conv_ln_g_l, conv_ln_b_l, w_conv_out_l)
    y_ctx = jnp.concatenate([yA_ctx, yB_ctx, yC_ctx, yD_ctx], axis=-1) @ w_out_l
    return y_lat, y_ctx

def setup_inputs(seed: int = 0) -> dict:
    key = jax.random.key(seed)
    ks = jax.random.split(key, 28)
    L, D = DEPTH, D_MODEL

    def nrm(k, shape, s):
        return jax.random.normal(k, shape, jnp.float32) * s

    def gain(k, shape):
        return 1.0 + 0.1 * jax.random.normal(k, shape, jnp.float32)

    return {
        'x': nrm(ks[0], (BATCH, SEQ, D), 1.0),
        'c': nrm(ks[1], (BATCH, D), 1.0),
        'ctx': nrm(ks[2], (BATCH, CTX_LEN, D), 1.0),
        'c_ctx': nrm(ks[3], (D,), 1.0),
        'w_ada': nrm(ks[4], (L, D, 6 * D), 0.5 * D ** -0.5),
        'b_ada': nrm(ks[5], (L, 6 * D), 0.02),
        'g_pre_mix': gain(ks[6], (L, D)),
        'g_post_mix': gain(ks[7], (L, D)),
        'g_pre_ffn': gain(ks[8], (L, D)),
        'g_post_ffn': gain(ks[9], (L, D)),
        'w_in': nrm(ks[10], (L, D, IN_COLS), D ** -0.5),
        'w_out': nrm(ks[11], (L, MIX_WIDTH, D), MIX_WIDTH ** -0.5),
        'lam_q1': nrm(ks[12], (L, A_DQK), 0.1),
        'lam_k1': nrm(ks[13], (L, A_DQK), 0.1),
        'lam_q2': nrm(ks[14], (L, A_DQK), 0.1),
        'lam_k2': nrm(ks[15], (L, A_DQK), 0.1),
        'g_subln': gain(ks[16], (L, A_DV)),
        'w_pool': nrm(ks[17], (L, C_GROUPS, C_GW, C_GW), C_GW ** -0.5),
        's_pool': 0.5 + 0.1 * jax.random.normal(ks[18], (L, C_WIDTH), jnp.float32),
        'conv_w': nrm(ks[19], (L, CONV_K, 1, D_WIDTH), CONV_K ** -0.5),
        'conv_b': nrm(ks[20], (L, D_WIDTH), 0.02),
        'conv_ln_g': gain(ks[21], (L, D_WIDTH)),
        'conv_ln_b': nrm(ks[22], (L, D_WIDTH), 0.02),
        'w_conv_out': nrm(ks[23], (L, D_WIDTH, D_WIDTH), D_WIDTH ** -0.5),
        'w_ffn_gate': nrm(ks[24], (L, D, D_FF), D ** -0.5),
        'w_ffn_up': nrm(ks[25], (L, D, D_FF), D ** -0.5),
        'w_ffn_down': nrm(ks[26], (L, D_FF, D), D_FF ** -0.5),
    }

def reference(x, c, ctx, c_ctx, w_ada, b_ada, g_pre_mix, g_post_mix, g_pre_ffn, g_post_ffn,
              w_in, w_out, lam_q1, lam_k1, lam_q2, lam_k2, g_subln, w_pool, s_pool,
              conv_w, conv_b, conv_ln_g, conv_ln_b, w_conv_out, w_ffn_gate, w_ffn_up, w_ffn_down):
    t_len = x.shape[1]
    ROWS = t_len // GRID_W
    row = jnp.repeat(jnp.arange(ROWS, dtype=jnp.int32), GRID_W)
    col = jnp.tile(jnp.arange(GRID_W, dtype=jnp.int32), ROWS)
    rope_a = _axial_rope(row, col, A_DQK, x.dtype)
    rope_b = _axial_rope(row, col, B_DK, x.dtype)
    sc = jax.nn.silu(c)
    scc = jax.nn.silu(c_ctx)
    h_lat, h_ctx = x, ctx
    for l in range(DEPTH):
        last = l == DEPTH - 1
        mod_lat = (sc @ w_ada[l] + b_ada[l])[:, None, :]
        mod_ctx = (scc @ w_ada[l] + b_ada[l])[None, None, :]
        sm, cm, gm, sf, cf, gf = jnp.split(mod_lat, 6, axis=-1)
        sm_c, cm_c, gm_c, sf_c, cf_c, gf_c = jnp.split(mod_ctx, 6, axis=-1)
        lam_init = 0.8 - 0.6 * math.exp(-0.3 * l)
        lam = (jnp.exp(jnp.sum(lam_q1[l] * lam_k1[l]).astype(jnp.float32))
               - jnp.exp(jnp.sum(lam_q2[l] * lam_k2[l]).astype(jnp.float32)) + lam_init)

        u_lat = _modulate(_rms_norm(h_lat, g_pre_mix[l]), sm, cm)
        u_ctx = _modulate(_rms_norm(h_ctx, g_pre_mix[l]), sm_c, cm_c)
        y_lat, y_ctx = _mixing(u_lat, u_ctx, w_in[l], w_out[l], lam, lam_init, g_subln[l],
                               w_pool[l], s_pool[l], conv_w[l], conv_b[l], conv_ln_g[l],
                               conv_ln_b[l], w_conv_out[l], rope_a, rope_b, last)
        h_lat = h_lat + gm * _rms_norm(y_lat, g_post_mix[l])
        f_lat = _swiglu(_modulate(_rms_norm(h_lat, g_pre_ffn[l]), sf, cf),
                        w_ffn_gate[l], w_ffn_up[l], w_ffn_down[l])
        h_lat = h_lat + gf * _rms_norm(f_lat, g_post_ffn[l])
        if not last:
            h_ctx = h_ctx + gm_c * _rms_norm(y_ctx, g_post_mix[l])
            f_ctx = _swiglu(_modulate(_rms_norm(h_ctx, g_pre_ffn[l]), sf_c, cf_c),
                            w_ffn_gate[l], w_ffn_up[l], w_ffn_down[l])
            h_ctx = h_ctx + gf_c * _rms_norm(f_ctx, g_post_ffn[l])
    return h_lat


_drawn_inputs = setup_inputs


def setup_inputs(seed=0):
    import zlib

    import numpy as np

    out = dict(_drawn_inputs(seed))
    spreads = {}
    factors = {'lam_q1': 26.857,
     'lam_k1': 5.361,
     'lam_q2': 8.0,
     'lam_k2': 200.0,
     'conv_b': 8.0,
     'conv_ln_g': 2.724,
     'conv_ln_b': 35.899,
     'g_subln': 3.816,
     's_pool': 3.522}
    for name, (base, spread) in spreads.items():
        noise = np.random.default_rng([zlib.crc32(name.encode()), seed]).standard_normal(out[name].shape)
        drawn = base * np.exp(spread * noise) if base else spread * noise
        out[name] = jnp.asarray(drawn.astype(out[name].dtype))
    for name, factor in factors.items():
        out[name] = (out[name] * factor).astype(out[name].dtype)
    return out
```

```python
import math
from contextlib import ExitStack

import numpy as np

import concourse.bass as bass
from concourse import mybir

ALU = mybir.AluOpType
ACT = mybir.ActivationFunctionType
AX = mybir.AxisListType
F32 = mybir.dt.float32
F16 = mybir.dt.float16

P = 128
D = 1024
KD = D // P
LAYERS = 2
CTX, LAT = 256, 1024
TOK = CTX + LAT
NTILE = TOK // P
CT = CTX // P
DFF = 2816
NF = DFF // P
FPARTS = (8, 8, 6)
NIN = 22
HA, DQ, DV = 4, 32, 64
HB, DK = 4, 64
TAPS, HALF = 31, 15
PADW = HALF + CTX + HALF + LAT + HALF
SEG = ((HALF, 0, CTX), (2 * HALF + CTX, CTX, LAT))
WS, XS = 64.0, 16.0
UNS = 1.0 / (WS * XS)
H, U, G, Y = 0, 8, 16, 24
CD_UNITS, B_UNITS, A_UNITS = 6, 10, 6
LAYER_UNITS = NIN + KD + 2 * NF + KD * len(FPARTS)
LAM_INIT = [0.8 - 0.6 * math.exp(-0.3 * l) for l in range(LAYERS)]
LOG_GAMMA = [math.log(1.0 - 2.0 ** (-5 - h)) for h in range(HB)]
SCORE = DQ ** -0.5 / (XS * XS)
SMALLS = {"g_pre": KD * 2, "g_post": KD * 2, "conv_w": 2 * TAPS, "conv_b": 2, "ln_g": 2, "ln_b": 2,
          "s_pool": 2, "g_sub": 1}
SM_AT = {}
_at = 0
for _k, _n in SMALLS.items():
    SM_AT[_k] = (_at, _n)
    _at += _n
SM_W = _at


def spans(t0):
    return [(a, min(a + 512, TOK)) for a in range(t0, TOK, 512)]


class Chain:

    def __init__(self, eng, s):
        self.eng, self.s, self.base, self.k = eng, s, 0, 0

    def link(self, ins):
        ins.then_inc(self.s, 1)
        self.k += 1
        self.eng.wait_ge(self.s, self.base + self.k)

    def enter(self, r, per):
        self.outer = self.base + self.k
        self.base, self.k = self.outer + r * per, 0

    def leave(self, n, per):
        assert self.k == per, (self.k, per)
        self.base, self.k = self.outer + n * per, 0


def build(nc, a, out):
    with ExitStack() as ctx:
        def sb(name, shape, dt=F32):
            return ctx.enter_context(nc.sbuf_tensor(name, shape, dt))

        def sem(name):
            return ctx.enter_context(nc.semaphore(name))

        R = sb("R", [P, 32, TOK])
        X = sb("X", [P, 4 * PADW])
        stage = sb("stage", [P, 2, KD, P])
        whi = sb("whi", [P, 2, KD, P], F16)
        wlo = sb("wlo", [P, 2, KD, P], F16)
        ident = sb("ident", [P, P])
        ones = sb("ones", [P, P])
        perm = sb("perm", [P, P])
        blockm = sb("blockm", [P, P])
        SW = sb("SW", [P, 768])
        T = sb("T", [P, 1024])
        small = sb("small", [P, LAYERS, SM_W])
        rtab = sb("rtab", [P, 18])
        vec = sb("vec", [P, LAYERS, 3, 2, 2, KD])
        csil = sb("csil", [P, KD, 2])
        lamv = sb("lamv", [P, 16])
        tiny = sb("tiny", [P, 36])
        nhalf = tiny[:, 0:1]
        epsv = tiny[:, 1:3]
        smax = tiny[:, 4:8].rearrange("p (b c) -> p b c", b=2)
        nbias = tiny[:, 8:12].rearrange("p (b c) -> p b c", b=2)
        den = tiny[:, 12:16].rearrange("p (b c) -> p b c", b=2)
        beta = tiny[:, 16:18]
        rl = tiny[:, 20:24]
        st8 = sb("st8", [P, 4, 8])
        PS = ctx.enter_context(nc.psum_tensor("PS", [P, 8, 512], F32))

        R16 = R[:, :, :].rearrange("p r t -> p (r t)").bitcast(F16).rearrange("p (r t) -> p r t", r=32)
        PSF = PS[:, :, :].rearrange("p b t -> p (b t)")

        def hl(row, part, c0, c1):
            return R16[:, row, part * TOK + c0:part * TOK + c1]

        def hlr(row, n, part, c0, w):
            return R16[:, row:row + n, bass.ds(part * TOK + c0, w)]

        def slot(s, t0=0):
            return PSF[:, 1536 * s:1536 * s + TOK - t0]

        def sm(l, k, i=0, n=1):
            at = SM_AT[k][0] + i
            return small[:, l, at:at + n]

        def vv(l, kind, norm, stream, d):
            return vec[:, l, kind, norm, stream, d:d + 1]

        def xrow(i):
            return X[:, i * PADW:i * PADW + TOK]

        Xpad = X[:, :].rearrange("p (r t) -> p r t", r=4)
        Gpad = R[:, G:G + 7, :].rearrange("p r t -> p (r t)")[:, 0:6 * PADW].rearrange("p (r t) -> p r t", r=6)
        vtok = X[:, 0:NTILE * 256].rearrange("p (t c) -> p t c", c=256)
        Vst = X[:, 0:NTILE * 256].bitcast(F16).rearrange("p (t h x e) -> p t h x e", t=NTILE, h=HA, x=2)
        Sb = X[:, 2 * PADW:2 * PADW + NTILE * 256].rearrange("p (t c) -> p t c", c=256)
        wpw = SW[:, 0:512].rearrange("p (k e) -> p k e", k=2)
        wpool = SW[:, 512:768].rearrange("p (k e) -> p k e", k=2)
        stk = SW[:, :].bitcast(F16)[:, 0:4 * 352].rearrange("p (j c) -> p j c", j=4)
        Kst = R16[:, G:G + 4, :].rearrange("p r t -> p (r t)").rearrange("p (h t) -> p h t", h=8)
        Qst = R16[:, G + 4:G + 8, :].rearrange("p r t -> p (r t)").rearrange("p (h t) -> p h t", h=8)
        RB = R[:, 18:20, :].rearrange("p r t -> p (r t)")
        dmask = RB[:, 0:1024].rearrange("p (d h c) -> p d h c", d=2, h=HB)
        pmask = RB[:, 1024:2048].rearrange("p (d h c) -> p d h c", d=2, h=HB)
        ysum = RB[:, 2048:2560]
        P1 = [R[:, U + i, :] for i in range(2)]
        P2 = [R[:, U + 2 + i, :] for i in range(2)]
        Wt = [R[:, U + 4 + i, :] for i in range(2)]
        WTb = R16[:, U + 6, 0:2048].rearrange("p (b x c) -> p b x c", b=2, x=2)
        AO = R[:, U + 7, 0:1024].rearrange("p (i h e) -> p i h e", i=4, h=HA)

        cross = rtab[:, 0:8]
        wend = rtab[:, 8:16]
        g128 = rtab[:, 16:18]

        PER_LAYER = dict(
            cd_tab=64, pads_zero=1, glu=2, conv=TAPS * 4, pooled=2, pool_ps=6, pool_hi=6, pool_done=6,
            mean_ps=1, centered=2, cd_sq=2, var_ps=1, ln_root=1, zed=2, zed_tanh=2, silu=2, pw_ps=6, pw_hi=6, pw_done=6,
            b_tab=32, gate_tanh=4, roped_ps=4, roped=4, d_tab=16,
            tr_ps=NTILE, v_tok=NTILE, k_tok=NTILE, vw=NTILE - 1, kv_ps=NTILE - 1, state=NTILE,
            tr2_ps=NTILE - 1, k_tok2=NTILE - 1, vw2=NTILE - 1, kv2_ps=NTILE - 1, state2=NTILE,
            sc_ps=NTILE, masked=NTILE, y_ps=NTILE, y_mid=NTILE, y_sq=NTILE, y_var=NTILE, y_pow=NTILE, y_norm=NTILE,
            yt_ps=NTILE, yb_sum=NTILE, yb_hi=NTILE, yb_done=NTILE,
            a_tab=64, perm_ps=12, rot=12, rot_hi=12, rot_lo=12, stk_ps=48, stk_done=48,
            vt_ps=NTILE, vt_hi=NTILE, vt_done=NTILE, g_tanh=NF, ffn_hi=NF, ffn_lo=NF)
        S = {n: sem(n) for n in
             ("consts smalls csil c_tanh lam_dots lam_exp ada_used vec_ready small_const w_hi w_lo units "
              "slot_free act_own dve_own pool_own h_in out_done sq_ready sq_used sumsq root u_scaled u_hi u_done h_rows").split()}
        S |= {n: sem(n) for n in PER_LAYER}
        ada_landed = [sem(f"ada_landed{i}") for i in range(8)]
        w_landed = [sem(f"w_landed{j}") for j in range(2)]
        for l in range(LAYERS):
            for run in (("c", "l") if l < LAYERS - 1 else ("l",)):
                for n in "scores nbias exps w wt_ps wt_hi wt_lo pv o_lo o_sum o_var o_pow o_norm ot_ps ot_hi ot_done".split():
                    S[f"{n}_{run}{l}"] = sem(f"{n}_{run}_{l}")

        def at(name, l):
            return PER_LAYER[name] * l

        def unit0(l, stage, part=0):
            at = l * LAYER_UNITS
            if stage == "in":
                return at
            at += NIN
            if stage == "out":
                return at
            at += KD
            for q in range(part):
                at += 2 * FPARTS[q] + KD
            return at if stage == "gu" else at + 2 * FPARTS[part]

        def gemm_list():
            out_ = []
            for l in range(LAYERS):
                out_ += [8] * (NIN + KD)
                for f in FPARTS:
                    out_ += [8] * (2 * f) + [f] * KD
            return out_
        UK = gemm_list()
        assert len(UK) == LAYERS * LAYER_UNITS

        def row_lat(l, after_mix=True):
            return CTX if l == LAYERS - 1 else 0

        block = ctx.enter_context(nc.Block())

        B_ORDER = [1, 0] + list(range(NTILE - 1, CT - 1, -1))

        def first_tok(l):
            return CTX if l == LAYERS - 1 else 0

        def segs(l):
            return SEG[1:] if first_tok(l) else SEG

        def streams(t0):
            return [(0, CTX, TOK)] if t0 else [(1, 0, CTX), (0, CTX, TOK)]

        def attend_runs(l):
            runs = [("l", CT, NTILE - CT, NTILE)]
            return runs if first_tok(l) else [("c", 0, CT, CT)] + runs

        def key_groups(nk):
            return [(g, min(4, nk - g)) for g in range(0, nk, 4)]

        def pairs(eng, n, body, start=0):
            for i in range(2 * start):
                body(i, i, 0)
            if n > 2 * start + 2:
                with eng.Fori(start, n // 2 - 1) as r:
                    for j in range(2):
                        body(2 * r + j, j, r)
            for j in range(2):
                body(n - 2 + j, j, n // 2 - 1)

        @block.sync
        def _(sp):
            for name, dst in (("ident", ident), ("ones", ones), ("blockm", blockm), ("rtab", rtab)):
                sp.dma_start(dst[:, :], a[name]).then_inc(S["consts"], 16)
            sp.dma_start(small[:, :, :], a["small"]).then_inc(S["smalls"], 16)
            sp.dma_start(csil[:, :, :], a["c2"]).then_inc(S["smalls"], 16)
            sp.dma_start(T[:, 0:256], a["lam"]).then_inc(S["smalls"], 16)
            sp.dma_start(R[:, Y + 7, 0:LAYERS * 48], a["b_ada"]).then_inc(S["smalls"], 16)

            def ada_slot(i):
                return R[:, G + i, 0:1024].rearrange("p (k m) -> p k m", k=KD)

            for i in range(8):
                sp.dma_start(ada_slot(i), a["w_ada"][i]).then_inc(ada_landed[i], 16)
            for d in range(KD):
                sp.dma_start(R[:, H + d, :], a["x"][d]).then_inc(S["h_in"], 16)
            with sp.Fori(1, LAYERS * 6) as r:
                for i in range(8):
                    sp.wait_ge(S["ada_used"], 8 * r + (i - 7))
                    sp.dma_start(ada_slot(i), a["w_ada"][bass.ds(8 * r + i, 1)].rearrange("a p k m -> p (a k) m")
                                 ).then_inc(ada_landed[i], 16)

            def stream(u0, n, K, src):
                start = 0
                if u0 == 0:
                    for j in range(2):
                        sp.dma_start(stage[:, j, 0:K, :], src[j]).then_inc(w_landed[j], 16)
                    start = 1
                if start == n // 2:
                    return
                with sp.Fori(start, n // 2) as r:
                    for j in range(2):
                        sp.wait_ge(S["w_lo"], 2 * r + (u0 + j - 1))
                        sp.dma_start(stage[:, j, 0:K, :], src[bass.ds(2 * r + j, 1)].rearrange("a p k m -> p (a k) m")
                                     ).then_inc(w_landed[j], 16)

            for l in range(LAYERS):
                stream(unit0(l, "in"), 2, KD, a["w_in"][l][0:2])
                if l:
                    sp.wait_ge(S["h_rows"], 2 * KD * l)
                    sp.wait_ge(S["stk_ps"], at("stk_ps", l-1) + 4 * 2 * (len(spans(0)) + len(spans(first_tok(l - 1)))))
                for j in range(2):
                    sp.dma_start(R[:, Y + j, :], a["cnt"][j]).then_inc(S["cd_tab"], 16)
                sp.dma_start(SW[:, :], a["swb"][l]).then_inc(S["cd_tab"], 16)
                sp.dma_start(perm[:, :], a["permB"]).then_inc(S["cd_tab"], 16)
                ahead = CD_UNITS + B_UNITS + 2
                stream(unit0(l, "in") + 2, ahead - 2, KD, a["w_in"][l][2:ahead])
                sp.wait_ge(S["silu"], at("silu", l) + 2)
                for j in range(2):
                    sp.dma_start(xrow(2 + j), a["ropeB"][j]).then_inc(S["b_tab"], 16)
                sp.wait_ge(S["tr_ps"], at("tr_ps", l) + NTILE)
                sp.dma_start(RB[:, 0:1024], a["dmask"]).then_inc(S["d_tab"], 16)
                sp.wait_ge(S["yb_done"], at("yb_done", l) + NTILE - first_tok(l) // P)
                for j in range(2):
                    sp.dma_start(xrow(2 + j), a["ropeA"][j]).then_inc(S["a_tab"], 16)
                sp.dma_start(SW[:, 0:704], a["stk"]).then_inc(S["a_tab"], 16)
                sp.dma_start(perm[:, :], a["permA"]).then_inc(S["a_tab"], 16)
                stream(unit0(l, "in") + ahead, NIN - ahead, KD, a["w_in"][l][ahead:NIN])
                stream(unit0(l, "out"), KD, KD, a["w_out"][l])
                f0 = 0
                for q, nf in enumerate(FPARTS):
                    stream(unit0(l, "gu", q), 2 * nf, KD, a["w_gu"][l][2 * f0:2 * (f0 + nf)])
                    stream(unit0(l, "down", q), KD, nf, a[f"w_down{q}"][l])
                    f0 += nf
            for d in range(KD):
                sp.wait_ge(S["h_rows"], 2 * KD * LAYERS - KD + d + 1)
                sp.dma_start(out[d], R[:, H + d, CTX:TOK]).then_inc(S["out_done"], 16)
            sp.wait_ge(S["out_done"], 16 * KD)

        @block.tensor
        def _(pe):
            mm = nc.tensor.matmul

            def gemm_unit(u, j, K, row0, t0):
                pe.wait_ge(S["w_lo"], u + 1)
                if not (isinstance(u, int) and u < 2):
                    pe.wait_ge(S["slot_free"], u - 1)
                for c0, c1 in spans(t0):
                    o = slot(j, t0)[:, c0 - t0:c1 - t0]
                    for k in range(K):
                        for q, (w, part) in enumerate(((whi, 0), (whi, 1), (wlo, 0))):
                            last = mm(o, w[:, j, k, :], hl(row0 + k, part, c0, c1),
                                      start=(k == 0 and q == 0), stop=(k == K - 1 and q == 2))
                last.then_inc(S["units"], 1)

            def gemm(u0, n, K, row0, t0):
                pairs(pe, n, lambda i, j, r: gemm_unit(i + u0, j, K, row0, t0), start=int(u0 == 0))

            def sum_rows(inst, t0):
                pe.wait_ge(S["sq_used"], KD * (inst + 1))
                for c0, c1 in spans(t0):
                    last = mm(slot(0, t0)[:, c0 - t0:c1 - t0], ones[:, :], xrow(0)[:, c0:c1], start=True, stop=True)
                last.then_inc(S["sumsq"], 1)

            def attend(l, run, t_first, nt, nk):
                s = lambda n: S[f"{n}_{run}{l}"]
                groups = key_groups(nk)
                NG, keys = len(groups), nk * P

                def scores(r, h):
                    n = 4 * r + h
                    for c in range(2):
                        if not (isinstance(r, int) and n == 0):
                            pe.wait_ge(s("exps"), 2 * n + (c - 1))
                        for k0 in range(0, keys, 512):
                            k1 = min(k0 + 512, keys)
                            last = mm(slot(c)[:, k0:k1], Qst[:, 2 * h + c, bass.ds((t_first + r) * P, P)],
                                      Kst[:, 2 * h + c, k0:k1], start=True, stop=True)
                        last.then_inc(s("scores"), 1)

                def mix(r, h):
                    n = 4 * r + h

                    def turn(g):
                        k0, m = groups[g]
                        if g == 0:
                            pe.wait_ge(s("w"), n + 1)
                        if not (isinstance(r, int) and NG * n + g == 0):
                            pe.wait_ge(s("wt_lo"), NG * n + g)
                        for i in range(m):
                            last = nc.tensor.transpose(PS[:, 6, i * P:(i + 1) * P],
                                                       Wt[h % 2][:, (k0 + i) * P:(k0 + i + 1) * P], ident[:, :])
                        last.then_inc(s("wt_ps"), 1)

                    def values(g):
                        k0, m = groups[g]
                        pe.wait_ge(s("wt_lo"), NG * n + (g + 1))
                        if g == 0 and h == 0 and not (isinstance(r, int) and r == 0):
                            pe.wait_ge(s("o_sum"), r)
                        for i in range(m):
                            for x in range(2):
                                last = mm(PS[:, 7, h * P:(h + 1) * P],
                                          WTb[:, (NG * h + g) % 2, x, i * P:(i + 1) * P],
                                          Vst[:, k0 + i, h, :, :],
                                          start=(k0 + i == 0 and x == 0), stop=(k0 + i == nk - 1 and x == 1))
                        last.then_inc(s("pv"), 1)

                    if h == 1 and not (isinstance(r, int) and r == 0):
                        pe.wait_ge(s("ot_done"), r)
                    for g in range(NG):
                        turn(g)
                        if g:
                            values(g - 1)
                    values(NG - 1)

                def turn_out(r):
                    pe.wait_ge(s("o_norm"), r + 1)
                    if not (isinstance(r, int) and r == nt - 1):
                        pe.wait_ge(s("wt_lo"), NG * (4 * r + 5))
                    for j in range(2):
                        last = nc.tensor.transpose(PS[:, 6, j * P:(j + 1) * P],
                                                   AO[:, 3, :, :].rearrange("p h e -> p (h e)")[:, j * P:(j + 1) * P],
                                                   ident[:, :])
                    last.then_inc(s("ot_ps"), 1)

                def tile(r, first=False):
                    for h in range(HA):
                        scores(r, h)
                        if h:
                            mix(r, h - 1)
                            if h == 1 and not first:
                                turn_out(r - 1)
                        elif not first:
                            mix(r - 1, HA - 1)

                tile(0, first=True)
                with pe.Fori(1, nt) as r:
                    tile(r)
                mix(nt - 1, HA - 1)
                turn_out(nt - 1)

            pe.wait_ge(S["csil"], 1)
            with pe.Fori(0, LAYERS * 6) as r:
                for i in range(8):
                    pe.wait_ge(ada_landed[i], 16 * r + 16)
                    for k in range(KD):
                        last = mm(PSF[:, bass.ds(16 * r + (3072 + 2 * i), 2)], R[:, G + i, k * P:(k + 1) * P],
                                  csil[:, k, :], start=(k == 0), stop=(k == KD - 1))
                    last.then_inc(S["ada_used"], 1)
            pe.wait_ge(S["consts"], 64)
            sum_rows(0, 0)

            for l in range(LAYERS):
                t0 = first_tok(l)
                sp0 = spans(t0)
                u0 = unit0(l, "in")
                pe.wait_ge(S["u_done"], 2 * KD * l + KD)
                pe.wait_ge(S["root"], 4 * l + 1)
                gemm(u0, CD_UNITS, KD, U, t0)
                gemm(u0 + 6, 4, KD, U, 0)
                gemm(u0 + 10, 6, KD, U, t0)
                pe.wait_ge(S["cd_tab"], at("cd_tab", l) + 64)
                pe.wait_ge(S["pooled"], at("pooled", l) + 2)
                for j in range(2):
                    for c, (c0, c1) in enumerate(sp0):
                        n = j * len(sp0) + c
                        if n >= 2:
                            pe.wait_ge(S["pool_done"], at("pool_done", l) + n - 1)
                        mm(PS[:, 6 + n % 2, 0:c1 - c0], wpool[:, j, :], R[:, Y + 2 + j, c0:c1],
                           start=True, stop=True).then_inc(S["pool_ps"], 1)
                nconv = TAPS * 2 * len(segs(l))
                pe.wait_ge(S["conv"], at("conv", l) + nconv)
                pe.wait_ge(S["slot_free"], u0 + 16)
                for c0, c1 in sp0:
                    for j in range(2):
                        last = mm(slot(0, t0)[:, c0 - t0:c1 - t0], ones[:, :], R[:, Y + 6 + j, c0:c1],
                                  start=(j == 0), stop=(j == 1))
                last.then_inc(S["mean_ps"], 1)
                pe.wait_ge(S["cd_sq"], at("cd_sq", l) + 2)
                for c0, c1 in sp0:
                    for j in range(2):
                        last = mm(slot(1, t0)[:, c0 - t0:c1 - t0], ones[:, :], xrow(j)[:, c0:c1],
                                  start=(j == 0), stop=(j == 1))
                last.then_inc(S["var_ps"], 1)
                pe.wait_ge(S["silu"], at("silu", l) + 2)
                pe.wait_ge(S["pool_done"], at("pool_done", l) + 2 * len(sp0))
                for e in range(2):
                    for c, (c0, c1) in enumerate(sp0):
                        n = e * len(sp0) + c
                        if n >= 2:
                            pe.wait_ge(S["pw_done"], at("pw_done", l) + n - 1)
                        for k in range(2):
                            last = mm(PS[:, 6 + n % 2, 0:c1 - c0], wpw[:, k, e * P:(e + 1) * P], xrow(k)[:, c0:c1],
                                      start=(k == 0), stop=(k == 1))
                        last.then_inc(S["pw_ps"], 1)
                for i, row in enumerate((G, G + 1, G + 4, G + 5)):
                    tr = 0 if i < 2 else t0
                    if i >= 2:
                        pe.wait_ge(S["roped"], at("roped", l) + i - 1)
                    for c0, c1 in spans(tr):
                        last = mm(slot(i % 2, tr)[:, c0 - tr:c1 - tr], perm[:, :], R[:, row, c0:c1],
                                  start=True, stop=True)
                    last.then_inc(S["roped_ps"], 1)

                def tok_turn(i):
                    t = B_ORDER[i]
                    if i == 0:
                        pe.wait_ge(S["roped"], at("roped", l) + 4)
                        pe.wait_ge(S["pw_done"], at("pw_done", l) + 2 * len(sp0))
                    else:
                        pe.wait_ge(S["k_tok"], at("k_tok", l) + i)
                    for q, row in enumerate((G + 2, G + 3, G, G + 1)):
                        last = nc.tensor.transpose(PS[:, 6, q * P:(q + 1) * P], R[:, row, t * P:(t + 1) * P], ident[:, :])
                    last.then_inc(S["tr_ps"], 1)

                def backward_kv(i):
                    pe.wait_ge(S["vw"], at("vw", l) + i + 1)
                    pe.wait_ge(S["k_tok"], at("k_tok", l) + i + 1)
                    pe.wait_ge(S["state"], at("state", l) + i + 1)
                    for q in range(2):
                        last = mm(PS[:, 7, q * P:(q + 1) * P], T[:, (i % 2) * 256 + q * P:(i % 2) * 256 + (q + 1) * P],
                                  T[:, 512 + (i % 2) * 256 + q * P:512 + (i % 2) * 256 + (q + 1) * P],
                                  start=True, stop=True)
                    last.then_inc(S["kv_ps"], 1)

                tok_turn(0)
                for i in range(NTILE):
                    if i + 1 < NTILE:
                        tok_turn(i + 1)
                        backward_kv(i)

                tq = t0 // P

                def keys_and_scores(t):
                    if t == 0:
                        pe.wait_ge(S["k_tok"], at("k_tok", l) + NTILE)
                        pe.wait_ge(S["roped"], at("roped", l) + 4)
                    else:
                        pe.wait_ge(S["k_tok2"], at("k_tok2", l) + t)
                    if t < NTILE - 1:
                        for q in range(2):
                            last = nc.tensor.transpose(PS[:, 6, q * P:(q + 1) * P], R[:, G + q, t * P:(t + 1) * P],
                                                       ident[:, :])
                        last.then_inc(S["tr2_ps"], 1)
                    if t >= tq:
                        if t > tq:
                            pe.wait_ge(S["masked"], at("masked", l) + t - tq)
                        for h in range(HB):
                            b, q = 64 * (h % 2), h // 2
                            last = mm(PS[:, 4 * (h % 2), q * P:(q + 1) * P], R[b:b + 64, G + q, t * P:(t + 1) * P],
                                      R[b:b + 64, G + 4 + q, t * P:(t + 1) * P], start=True, stop=True)
                        last.then_inc(S["sc_ps"], 1)

                def retained_out(t):
                    n = t - tq
                    if n:
                        pe.wait_ge(S["y_mid"], at("y_mid", l) + n)
                    pe.wait_ge(S["masked"], at("masked", l) + n + 1)
                    for dr in range(2):
                        for h in range(HB):
                            mm(PS[:, 1, dr * 256 + h * 64:dr * 256 + (h + 1) * 64], pmask[:, dr, h, :],
                               vtok[:, t, h * 64:(h + 1) * 64], start=True, stop=True)
                    pe.wait_ge(S["state2"], at("state2", l) + t + 1)
                    for dr in range(2):
                        for q in range(2):
                            st = T[:, 512 + (t % 2) * 256 + q * P:512 + (t % 2) * 256 + (q + 1) * P] if dr == 0 \
                                else Sb[:, t, q * P:(q + 1) * P]
                            last = mm(PS[:, 2, dr * 256 + q * P:dr * 256 + (q + 1) * P],
                                      R[:, G + 4 + q, t * P:(t + 1) * P], st, start=True, stop=True)
                    last.then_inc(S["y_ps"], 1)

                keys_and_scores(0)
                for t in range(NTILE):
                    if t < NTILE - 1:
                        pe.wait_ge(S["vw2"], at("vw2", l) + t + 1)
                        pe.wait_ge(S["k_tok2"], at("k_tok2", l) + t + 1)
                        pe.wait_ge(S["state2"], at("state2", l) + t + 1)
                        for q in range(2):
                            last = mm(PS[:, 7, q * P:(q + 1) * P], T[:, q * P:(q + 1) * P],
                                      T[:, 256 + q * P:256 + (q + 1) * P], start=True, stop=True)
                        last.then_inc(S["kv2_ps"], 1)
                    if t >= tq:
                        retained_out(t)
                    if t < NTILE - 1:
                        keys_and_scores(t + 1)
                    if t >= tq:
                        pe.wait_ge(S["y_norm"], at("y_norm", l) + t - tq + 1)
                        if t > tq:
                            pe.wait_ge(S["yb_sum"], at("yb_sum", l) + t - tq)
                        for q in range(4):
                            last = nc.tensor.transpose(PS[:, 3, q * P:(q + 1) * P], ysum[:, q * P:(q + 1) * P], ident[:, :])
                        last.then_inc(S["yt_ps"], 1)

                tiles = [(0, 0), (1, 0), (0, t0), (1, t0)]
                pbase = 0

                def rotate_and_stack(i):
                    key, t_r = i < 2, tiles[i][1]
                    done = sum(len(spans(tiles[x][1])) for x in range(i))
                    ch = spans(t_r)

                    def partners(c):
                        c0, c1 = ch[c]
                        if c == 0:
                            pe.wait_ge(S["slot_free"], u0 + 16 + i + 1)
                        if done + c:
                            pe.wait_ge(S["rot"], at("rot", l) + done + c)
                        mm(PS[:, 6, 0:c1 - c0], perm[:, :], R[:, Y + i % 2, c0:c1],
                           start=True, stop=True).then_inc(S["perm_ps"], 1)

                    def stack(c):
                        c0, c1 = ch[c]
                        w = c1 - c0
                        pe.wait_ge(S["rot_lo"], at("rot_lo", l) + done + c + 1)
                        for j in range(4):
                            n = 4 * (done + c) + j
                            if n:
                                pe.wait_ge(S["stk_done"], at("stk_done", l) + n)
                            for x in range(2):
                                col = 192 + 32 * x if key else 64 * x
                                last = mm(PS[:, 7, 0:w], stk[:, j, col:col + P],
                                          hl(Y + i % 2, 0, 2 * c0 + x * w, 2 * c0 + (x + 1) * w),
                                          start=(x == 0), stop=(x == 1))
                            last.then_inc(S["stk_ps"], 1)

                    partners(0)
                    for c in range(len(ch)):
                        if c + 1 < len(ch):
                            partners(c + 1)
                        stack(c)

                pe.wait_ge(S["a_tab"], at("a_tab", l) + 64)
                pe.wait_ge(S["yb_sum"], at("yb_sum", l) + NTILE - tq)
                for i in range(A_UNITS):
                    gemm_unit(u0 + 16 + i, i % 2, KD, U, 0 if i < 2 or i >= 4 else t0)
                    if 1 <= i <= 4:
                        rotate_and_stack(i - 1)
                pe.wait_ge(S["slot_free"], u0 + NIN)
                pe.wait_ge(S["stk_done"], at("stk_done", l) + 4 * 2 * (len(spans(0)) + len(sp0)))
                for t in range(NTILE):
                    if t >= 2:
                        pe.wait_ge(S["vt_done"], at("vt_done", l) + t - 1)
                    for q in range(2):
                        last = nc.tensor.transpose(PS[:, 6 + t % 2, q * P:(q + 1) * P],
                                                   R[:, Y + q, t * P:(t + 1) * P], ident[:, :])
                    last.then_inc(S["vt_ps"], 1)
                pe.wait_ge(S["vt_done"], at("vt_done", l) + NTILE)
                pe.wait_ge(S["slot_free"], u0 + NIN)
                for run, t_first, nt, nk in attend_runs(l):
                    attend(l, run, t_first, nt, nk)
                    pe.wait_ge(S[f"ot_done_{run}{l}"], nt)

                gemm(unit0(l, "out"), KD, KD, Y, t0)
                pe.wait_ge(S["slot_free"], unit0(l, "out") + KD)
                sum_rows(4 * l + 1, t0)
                pe.wait_ge(S["root"], 4 * l + 2)
                sum_rows(4 * l + 2, t0)
                pe.wait_ge(S["u_done"], 2 * KD * (l + 1))
                for q, nf in enumerate(FPARTS):
                    gemm(unit0(l, "gu", q), 2 * nf, KD, U, t0)
                    pe.wait_ge(S["ffn_lo"], at("ffn_lo", l) + sum(FPARTS[:q + 1]))
                    gemm(unit0(l, "down", q), KD, nf, G, t0)
                pe.wait_ge(S["slot_free"], unit0(l + 1, "in"))
                sum_rows(4 * l + 3, t0)
                if l < LAYERS - 1:
                    pe.wait_ge(S["root"], 4 * l + 4)
                    sum_rows(4 * l + 4, t0)

        @block.scalar
        def _(act):
            A = nc.scalar.activation
            own = Chain(act, S["act_own"])

            def hi_part(v, j, K):
                act.wait_ge(w_landed[j], 8 * v + (16 - 8 * j))
                if not (isinstance(v, int) and v < 2):
                    act.wait_ge(S["units"], v - 1)
                A(whi[:, j, 0:K, :], stage[:, j, 0:K, :], ACT.Copy, scale=WS).then_inc(S["w_hi"], 1)

            def units(u0, n, evac):
                def body(i, j, r):
                    nxt = u0 + i + 1
                    if isinstance(i, int):
                        if nxt < len(UK):
                            hi_part(nxt, 1 - j, UK[nxt])
                    else:
                        hi_part(nxt, 1 - j, UK[u0 + 1])
                    act.wait_ge(S["units"], nxt)
                    evac(i, j, r)
                pairs(act, n, body)

            def root(inst, t0):
                act.wait_ge(S["sumsq"], inst + 1)
                A(xrow(1)[:, t0:], slot(0, t0), ACT.Sqrt, scale=1.0 / D, bias=epsv[:, 0:1]).then_inc(S["root"], 1)

            def squares_of_h(inst, t0, first_rows):
                for d in range(KD):
                    q = KD * inst + d
                    act.wait_ge(S["h_rows"], first_rows + d + 1)
                    act.wait_ge(S["sq_used"], q - 1)
                    A(xrow(2 + d % 2)[:, t0:], R[:, H + d, t0:], ACT.Square).then_inc(S["sq_ready"], 1)

            def modulate(l, norm, t0):
                for d in range(KD):
                    act.wait_ge(S["u_scaled"], KD * (2 * l + norm) + d + 1)
                    row = xrow(2 + d % 2)
                    for st, c0, c1 in streams(t0):
                        last = A(row[:, c0:c1], row[:, c0:c1], ACT.Identity,
                                 scale=vv(l, 0, norm, st, d), bias=vv(l, 1, norm, st, d))
                    own.link(last)
                    A(hl(U + d, 0, t0, TOK), row[:, t0:], ACT.Copy).then_inc(S["u_hi"], 1)

            def attend(l, run, t_first, nt, nk):
                s = lambda n: S[f"{n}_{run}{l}"]
                groups = key_groups(nk)
                NG, keys = len(groups), nk * P

                def exps(r, h, c):
                    n = 4 * r + h
                    act.wait_ge(s("nbias"), 2 * n + (c + 1))
                    if not (isinstance(r, int) and n < 2):
                        act.wait_ge(s("w"), n - 1)
                    A((P1, P2)[c][h % 2][:, 0:keys], slot(c)[:, 0:keys], ACT.Exp, scale=SCORE,
                      bias=nbias[:, h % 2, c:c + 1], accum_out=den[:, h % 2, c:c + 1]).then_inc(s("exps"), 1)

                def wt_hi(r, h, g):
                    n = 4 * r + h
                    w = groups[g][1] * P
                    act.wait_ge(s("wt_ps"), NG * n + (g + 1))
                    if not (isinstance(r, int) and NG * n + g < 2):
                        act.wait_ge(s("pv"), NG * n + (g - 1))
                    A(WTb[:, (NG * h + g) % 2, 0, 0:w], PS[:, 6, 0:w], ACT.Copy).then_inc(s("wt_hi"), 1)

                def o_lo(r):
                    act.wait_ge(s("pv"), NG * (4 * r + 4))
                    A(AO[:, 0, :, :], PS[:, 7, :].rearrange("p (h e) -> p h e", h=HA)[:, :, DV:2 * DV],
                      ACT.Copy).then_inc(s("o_lo"), 1)

                def out_hi(r):
                    act.wait_ge(s("ot_ps"), r + 1)
                    A(hlr(Y, 2, 0, (t_first + r) * P, P), PS[:, 6, 0:256].rearrange("p (j t) -> p j t", j=2),
                      ACT.Copy, scale=sm(l, "g_sub")).then_inc(s("ot_hi"), 1)

                def tile(r, first=False):
                    for h in range(HA):
                        rr, hh = (r, h - 1) if h else (r - 1, HA - 1)
                        exps(r, h, 0)
                        if h or not first:
                            wt_hi(rr, hh, 0)
                        exps(r, h, 1)
                        if h or not first:
                            for g in range(1, NG):
                                wt_hi(rr, hh, g)
                            if h == 0:
                                o_lo(r - 1)
                            if h == 1 and not first:
                                out_hi(r - 1)

                tile(0, first=True)
                with act.Fori(1, nt) as r:
                    tile(r)
                for g in range(NG):
                    wt_hi(nt - 1, HA - 1, g)
                o_lo(nt - 1)
                out_hi(nt - 1)

            act.wait_ge(S["smalls"], 64)
            A(T[:, 768:784], csil[:, :, :].rearrange("p k s -> p (k s)"), ACT.Tanh, scale=0.5).then_inc(S["c_tanh"], 1)
            act.wait_ge(S["lam_dots"], 1)
            A(lamv[:, 4:8], lamv[:, 0:4], ACT.Exp).then_inc(S["lam_exp"], 1)
            act.wait_ge(S["h_in"], 16 * KD)
            for d in range(KD):
                if d >= 2:
                    act.wait_ge(S["sq_used"], d - 1)
                A(xrow(2 + d % 2), R[:, H + d, :], ACT.Square).then_inc(S["sq_ready"], 1)
            act.wait_ge(S["small_const"], 3)
            root(0, 0)
            hi_part(0, 0, UK[0])
            act.wait_ge(S["vec_ready"], 1)

            for l in range(LAYERS):
                t0 = first_tok(l)
                sp0 = spans(t0)
                u0 = unit0(l, "in")
                modulate(l, 0, t0 * 0)

                def cd_evac(i, j, r):
                    kind, dst = ((ACT.Copy, Gpad[:, 2 + j, :]), (ACT.Tanh, Gpad[:, j, :]), (ACT.Copy, Xpad[:, j, :]))[r]
                    for p0, c0, n in segs(l):
                        last = A(dst[:, p0:p0 + n], slot(j, t0)[:, c0 - t0:c0 - t0 + n], kind,
                                 scale=UNS if r == 0 else UNS * 0.5)
                    last.then_inc(S["slot_free"], 1)

                for r in range(CD_UNITS // 2):
                    for j in range(2):
                        u = u0 + 2 * r + j
                        hi_part(u + 1, 1 - j, KD)
                        act.wait_ge(S["units"], u + 1)
                        cd_evac(2 * r + j, j, r)

                act.wait_ge(S["glu"], at("glu", l) + 2)
                act.wait_ge(S["pooled"], at("pooled", l) + 2)
                units(u0 + 6, 4, lambda i, j, r: A(R[:, bass.ds(G + i, 1), :], slot(j), ACT.Copy,
                                                   scale=UNS).then_inc(S["slot_free"], 1))
                units(u0 + 10, 2, lambda i, j, r: A(R[:, G + 4 + i, t0:], slot(j, t0), ACT.Copy,
                                                    scale=UNS).then_inc(S["slot_free"], 1))
                units(u0 + 12, 4, lambda i, j, r: A(R[:, bass.ds(G + 6 + i, 1), t0:], slot(j, t0), ACT.Tanh,
                                                    scale=UNS * 0.5).then_inc(S["gate_tanh"], 1))

                for j in range(2):
                    for c, (c0, c1) in enumerate(sp0):
                        n = j * len(sp0) + c
                        act.wait_ge(S["pool_ps"], at("pool_ps", l) + n + 1)
                        A(hl(Y + 4 + j, 0, c0, c1), PS[:, 6 + n % 2, 0:c1 - c0], ACT.Copy,
                          scale=sm(l, "s_pool", j)).then_inc(S["pool_hi"], 1)
                for j in range(2):
                    act.wait_ge(S["centered"], at("centered", l) + j + 1)
                    A(xrow(j)[:, t0:], R[:, Y + 6 + j, t0:], ACT.Square).then_inc(S["cd_sq"], 1)
                act.wait_ge(S["var_ps"], at("var_ps", l) + 1)
                A(xrow(2)[:, t0:], slot(1, t0), ACT.Sqrt, scale=1.0 / 256, bias=epsv[:, 1:2]).then_inc(S["ln_root"], 1)
                for j in range(2):
                    act.wait_ge(S["zed"], at("zed", l) + j + 1)
                    A(xrow(j)[:, t0:], R[:, Y + 6 + j, t0:], ACT.Tanh, scale=0.5).then_inc(S["zed_tanh"], 1)
                for e in range(2):
                    for c, (c0, c1) in enumerate(sp0):
                        n = e * len(sp0) + c
                        act.wait_ge(S["pw_ps"], at("pw_ps", l) + n + 1)
                        A(hl(Y + 6 + e, 0, c0, c1), PS[:, 6 + n % 2, 0:c1 - c0], ACT.Copy,
                          scale=XS * 0.5).then_inc(S["pw_hi"], 1)

                for i in range(NTILE):
                    act.wait_ge(S["tr_ps"], at("tr_ps", l) + i + 1)
                    A(vtok[:, B_ORDER[i], :], PS[:, 6, 0:256], ACT.Copy).then_inc(S["v_tok"], 1)
                    if i >= 2:
                        act.wait_ge(S["kv_ps"], at("kv_ps", l) + i - 1)
                    A(T[:, (i % 2) * 256:(i % 2) * 256 + 256], PS[:, 6, 256:512], ACT.Copy).then_inc(S["k_tok"], 1)
                tq = t0 // P
                act.wait_ge(S["kv_ps"], at("kv_ps", l) + NTILE - 1)
                for t in range(NTILE):
                    if t < NTILE - 1:
                        act.wait_ge(S["tr2_ps"], at("tr2_ps", l) + t + 1)
                        if t:
                            act.wait_ge(S["kv2_ps"], at("kv2_ps", l) + t)
                        A(T[:, 0:256], PS[:, 6, 0:256], ACT.Copy).then_inc(S["k_tok2"], 1)
                    if t >= tq:
                        n = t - tq
                        act.wait_ge(S["y_mid"], at("y_mid", l) + n + 1)
                        A(SW[:, 0:512], ysum, ACT.Square).then_inc(S["y_sq"], 1)
                        act.wait_ge(S["yb_sum"], at("yb_sum", l) + n + 1)
                        A(hlr(Y + 2, 2, 0, t * P, P), SW[:, 0:256].rearrange("p (j t) -> p j t", j=2), ACT.Copy,
                          scale=XS * 0.5 * UNS).then_inc(S["yb_hi"], 1)

                tr = [0, 0, t0, t0, 0, 0]

                def stack_out(i):
                    ch = spans(tr[i])
                    done = sum(len(spans(tr[x])) for x in range(i))
                    dst = Kst if i < 2 else Qst
                    for c, (c0, c1) in enumerate(ch):
                        w = c1 - c0
                        act.wait_ge(S["rot"], at("rot", l) + done + c + 1)
                        A(hl(Y + i % 2, 0, 2 * c0, 2 * c0 + w), T[:, 512:512 + w], ACT.Copy).then_inc(S["rot_hi"], 1)
                        for j in range(4):
                            act.wait_ge(S["stk_ps"], at("stk_ps", l) + 4 * (done + c) + j + 1)
                            A(dst[:, 4 * (i % 2) + j, c0:c1], PS[:, 7, 0:w], ACT.Copy).then_inc(S["stk_done"], 1)

                for i in range(A_UNITS):
                    u = u0 + 16 + i
                    hi_part(u + 1, 1 - i % 2, KD)
                    act.wait_ge(S["units"], u + 1)
                    A(R[:, Y + i % 2, tr[i]:], slot(i % 2, tr[i]), ACT.Copy, scale=UNS * XS).then_inc(S["slot_free"], 1)
                    if 1 <= i <= 4:
                        stack_out(i - 1)
                for t in range(NTILE):
                    act.wait_ge(S["vt_ps"], at("vt_ps", l) + t + 1)
                    A(Vst[:, t, :, 0, :], PS[:, 6 + t % 2, 0:256].rearrange("p (h e) -> p h e", h=HA),
                      ACT.Copy).then_inc(S["vt_hi"], 1)
                for run, t_first, nt, nk in attend_runs(l):
                    attend(l, run, t_first, nt, nk)

                def out_evac(i, j, r):
                    act.wait_ge(S["sq_used"], i + (KD * (4 * l + 1) - 1))
                    A(xrow(2 + j)[:, t0:], slot(j, t0), ACT.Square, scale=UNS).then_inc(S["sq_ready"], 1)
                    A(R[:, bass.ds(U + i, 1), t0:], slot(j, t0), ACT.Copy, scale=UNS).then_inc(S["slot_free"], 1)

                units(unit0(l, "out"), KD, out_evac)
                root(4 * l + 1, t0)
                squares_of_h(4 * l + 2, t0, 2 * KD * l)
                root(4 * l + 2, t0)
                modulate(l, 1, t0)

                done = 0
                for q, nf in enumerate(FPARTS):
                    def ffn_evac(i, j, r):
                        if j == 0:
                            act.wait_ge(S["slot_free"], i + (unit0(l, "gu", q) - 1))
                            A(xrow(1)[:, t0:], slot(0, t0), ACT.Tanh, scale=UNS * 0.5).then_inc(S["g_tanh"], 1)
                        else:
                            act.wait_ge(S["slot_free"], i + (unit0(l, "gu", q) + 1))
                            A(hlr(G + r, 1, 0, t0, TOK - t0) if isinstance(r, int) else
                              R16[:, bass.ds(G + r, 1), t0:TOK], xrow(3)[:, t0:], ACT.Copy).then_inc(S["ffn_hi"], 1)

                    def down_evac(i, j, r):
                        if q == 0:
                            A(R[:, bass.ds(Y + i, 1), t0:], slot(j, t0), ACT.Copy, scale=UNS).then_inc(S["slot_free"], 1)
                        elif q == len(FPARTS) - 1:
                            act.wait_ge(S["slot_free"], i + (unit0(l, "down", q) + 1))
                            act.wait_ge(S["sq_used"], i + (KD * (4 * l + 3) - 1))
                            A(xrow(2 + j)[:, t0:], R[:, bass.ds(Y + i, 1), t0:], ACT.Square).then_inc(S["sq_ready"], 1)

                    units(unit0(l, "gu", q), 2 * nf, ffn_evac)
                    units(unit0(l, "down", q), KD, down_evac)
                    done += nf
                root(4 * l + 3, t0)
                if l < LAYERS - 1:
                    squares_of_h(4 * l + 4, t0, 2 * KD * l + KD)
                    root(4 * l + 4, t0)

        @block.vector
        def _(dve):
            TS, TT, STT = nc.vector.tensor_scalar, nc.vector.tensor_tensor, nc.vector.scalar_tensor_tensor
            RED = nc.vector.tensor_reduce
            own = Chain(dve, S["dve_own"])

            def lo_part(v, j, K):
                dve.wait_ge(S["w_hi"], v + 1)
                STT(wlo[:, j, 0:K, :], stage[:, j, 0:K, :], WS, whi[:, j, 0:K, :],
                    ALU.mult, ALU.subtract).then_inc(S["w_lo"], 1)

            def units(u0, n, evac, wait=True):
                def body(i, j, r):
                    nxt = u0 + i + 1
                    if isinstance(i, int):
                        if nxt < len(UK):
                            lo_part(nxt, 1 - j, UK[nxt])
                    else:
                        lo_part(nxt, 1 - j, UK[u0 + 1])
                    evac(i, j, r)
                pairs(dve, n, body)

            def inverse_root(inst, t0):
                dve.wait_ge(S["root"], inst + 1)
                own.link(nc.vector.reciprocal(xrow(1)[:, t0:], xrow(1)[:, t0:]))

            def scale_rows(l, norm, t0):
                base = KD * (2 * l + norm)
                def lo(d):
                    dve.wait_ge(S["u_hi"], base + d + 1)
                    TT(hl(U + d, 1, t0, TOK), xrow(2 + d % 2)[:, t0:], hl(U + d, 0, t0, TOK),
                       ALU.subtract).then_inc(S["u_done"], 1)
                for d in range(KD):
                    if d >= 2:
                        dve.wait_ge(S["u_done"], base + d - 1)
                    else:
                        dve.wait_ge(S["sq_used"], KD * (4 * l + 2 * norm + 1))
                    TT(xrow(2 + d % 2)[:, t0:], R[:, H + d, t0:], xrow(1)[:, t0:], ALU.mult).then_inc(S["u_scaled"], 1)
                    if d:
                        lo(d - 1)
                lo(KD - 1)

            def add_to_h(l, norm, row0, t0):
                TT(R[:, row0, t0:], R[:, row0, t0:], xrow(1)[:, t0:], ALU.mult).then_inc(S["dve_own"], 1)
                own.k += 1
                for d in range(KD):
                    mark = own.base + own.k
                    if d + 1 < KD:
                        TT(R[:, row0 + d + 1, t0:], R[:, row0 + d + 1, t0:], xrow(1)[:, t0:],
                           ALU.mult).then_inc(S["dve_own"], 1)
                        own.k += 1
                    dve.wait_ge(S["dve_own"], mark)
                    for st, c0, c1 in streams(t0):
                        last = STT(R[:, H + d, c0:c1], R[:, row0 + d, c0:c1], vv(l, 2, norm, st, d),
                                   R[:, H + d, c0:c1], ALU.mult, ALU.add)
                    last.then_inc(S["h_rows"], 1)

            def attend(l, run, t_first, nt, nk):
                s = lambda n: S[f"{n}_{run}{l}"]
                groups = key_groups(nk)
                NG, keys = len(groups), nk * P

                def maxima(r, h, c):
                    n = 4 * r + h
                    dve.wait_ge(s("scores"), 2 * n + (c + 1))
                    own.link(RED(smax[:, h % 2, c:c + 1], slot(c)[:, 0:keys], AX.X, ALU.max))
                    if not (isinstance(r, int) and n < 2):
                        dve.wait_ge(s("exps"), 2 * n + (c - 3))
                    TS(nbias[:, h % 2, c:c + 1], smax[:, h % 2, c:c + 1], -SCORE, lamv[:, 12 + l:13 + l] if c == 0 else None,
                       ALU.mult, ALU.add if c == 0 else ALU.bypass).then_inc(s("nbias"), 1)

                def wt_lo(r, h, g):
                    n = 4 * r + h
                    w = groups[g][1] * P
                    dve.wait_ge(s("wt_hi"), NG * n + (g + 1))
                    TT(WTb[:, (NG * h + g) % 2, 1, 0:w], PS[:, 6, 0:w], WTb[:, (NG * h + g) % 2, 0, 0:w],
                       ALU.subtract).then_inc(s("wt_lo"), 1)

                def combine(r, h):
                    n = 4 * r + h
                    dve.wait_ge(s("exps"), 2 * n + 2)
                    d1, d2 = den[:, h % 2, 0:1], den[:, h % 2, 1:2]
                    TS(rl[:, h:h + 1], d1, XS, None, ALU.mult)
                    own.link(nc.vector.reciprocal(beta[:, 1:2], d2))
                    own.link(STT(beta[:, 0:1], d1, lamv[:, 10 + l:11 + l], beta[:, 1:2], ALU.mult, ALU.mult))
                    STT(Wt[h % 2][:, 0:keys], P2[h % 2][:, 0:keys], beta[:, 0:1], P1[h % 2][:, 0:keys],
                        ALU.mult, ALU.add).then_inc(s("w"), 1)

                def out_sum(r):
                    dve.wait_ge(s("o_lo"), r + 1)
                    O = PS[:, 7, :].rearrange("p (h e) -> p h e", h=HA)[:, :, 0:DV]
                    TT(AO[:, 1, :, :], O, AO[:, 0, :, :], ALU.add).then_inc(s("o_sum"), 1)
                    dve.wait_ge(s("o_sum"), r + 1)
                    own.link(nc.vector.reciprocal(rl[:, :], rl[:, :]))
                    own.link(TT(AO[:, 1, :, :], AO[:, 1, :, :], rl[:, :].rearrange("p (h e) -> p h e", e=1).to_broadcast([P, HA, DV]), ALU.mult))
                    own.link(TT(AO[:, 2, :, :], AO[:, 1, :, :], AO[:, 1, :, :], ALU.mult))
                    own.link(RED(st8[:, 0, 0:4], AO[:, 2, :, :], AX.X, ALU.add))
                    TS(st8[:, 1, 0:4], st8[:, 0, 0:4], 1.0 / DV, 1e-5, ALU.mult, ALU.add).then_inc(s("o_var"), 1)

                def out_norm(r):
                    dve.wait_ge(s("o_pow"), r + 1)
                    TT(AO[:, 3, :, :], AO[:, 1, :, :], st8[:, 2, 0:4].rearrange("p (h e) -> p h e", e=1).to_broadcast([P, HA, DV]),
                       ALU.mult).then_inc(s("o_norm"), 1)

                def out_lo(r):
                    dve.wait_ge(s("ot_hi"), r + 1)
                    STT(hlr(Y, 2, 1, (t_first + r) * P, P), PS[:, 6, 0:256].rearrange("p (j t) -> p j t", j=2),
                        sm(l, "g_sub"), hlr(Y, 2, 0, (t_first + r) * P, P), ALU.mult, ALU.subtract).then_inc(s("ot_done"), 1)

                def tile(r, first=False):
                    per = 22 if first else 26
                    for h in range(HA):
                        rr, hh = (r, h - 1) if h else (r - 1, HA - 1)
                        maxima(r, h, 0)
                        if h == 1 and not first:
                            out_norm(r - 1)
                        if h or not first:
                            wt_lo(rr, hh, 0)
                        maxima(r, h, 1)
                        if h or not first:
                            for g in range(1, NG):
                                wt_lo(rr, hh, g)
                            if h == 0:
                                out_sum(r - 1)
                            if h == 1 and not first:
                                out_lo(r - 1)
                        combine(r, h)

                per = 4 * 4 + 4
                tile(0, first=True)
                with dve.Fori(1, nt) as r:
                    own.enter(r - 1, per)
                    tile(r)
                own.leave(nt - 1, per)
                for g in range(NG):
                    wt_lo(nt - 1, HA - 1, g)
                out_sum(nt - 1)
                out_norm(nt - 1)
                out_lo(nt - 1)

            dve.wait_ge(S["smalls"], 64)
            lamq = T[:, 0:256].rearrange("p (m x e) -> p m x e", m=4, x=2)
            own.link(TT(T[:, 256:384].rearrange("p (m e) -> p m e", m=4), lamq[:, :, 0, :], lamq[:, :, 1, :], ALU.mult))
            RED(lamv[:, 0:4], T[:, 256:384].rearrange("p (m e) -> p m e", m=4), AX.X, ALU.add).then_inc(S["lam_dots"], 1)
            dve.wait_ge(S["c_tanh"], 1)
            cs = csil[:, :, :].rearrange("p k s -> p (k s)")
            own.link(STT(cs, T[:, 768:784], 1.0, cs, ALU.add, ALU.mult))
            TS(cs, cs, 0.5, None, ALU.mult).then_inc(S["csil"], 1)
            dve.wait_ge(S["lam_exp"], 1)
            dve.wait_ge(S["lam_dots"], 1)
            e2 = lamv[:, 4:8].rearrange("p (l x) -> p l x", x=2)
            s2 = lamv[:, 0:4].rearrange("p (l x) -> p l x", x=2)
            own.link(TT(lamv[:, 8:10], e2[:, :, 0], e2[:, :, 1], ALU.subtract))
            own.link(TT(lamv[:, 14:16], s2[:, :, 0], s2[:, :, 1], ALU.max))
            for l in range(LAYERS):
                own.link(TS(lamv[:, 10 + l:11 + l], lamv[:, 8 + l:9 + l], -1.0, -LAM_INIT[l], ALU.mult, ALU.add))
                own.link(TS(sm(l, "g_sub"), sm(l, "g_sub"), XS * (1.0 - LAM_INIT[l]), None, ALU.mult))
                own.link(TS(sm(l, "s_pool", 0, 2), sm(l, "s_pool", 0, 2), XS, None, ALU.mult))
            own.link(TS(lamv[:, 12:14], lamv[:, 14:16], 0.0, -1.0, ALU.max, ALU.mult))
            lo_part(0, 0, UK[0])
            dve.wait_ge(S["ada_used"], LAYERS * 48)
            for l in range(LAYERS):
                mod = T[:, 384 + 96 * l:480 + 96 * l].rearrange("p (m d s) -> p m d s", m=6, s=2)
                own.link(TT(T[:, 384 + 96 * l:480 + 96 * l].rearrange("p (m s) -> p m s", s=2),
                            PSF[:, 3072 + 96 * l:3168 + 96 * l].rearrange("p (m s) -> p m s", s=2),
                            R[:, Y + 7, 48 * l:48 * l + 48].rearrange("p (m s) -> p m s", s=1).to_broadcast([P, 48, 2]), ALU.add))
                for n in range(2):
                    for st in range(2):
                        own.link(STT(vec[:, l, 0, n, st, :], mod[:, 3 * n + 1, :, st], 1.0,
                                     sm(l, "g_pre", KD * n, KD), ALU.add, ALU.mult))
                        own.link(TS(vec[:, l, 0, n, st, :], vec[:, l, 0, n, st, :], XS, None, ALU.mult))
                        own.link(TS(vec[:, l, 1, n, st, :], mod[:, 3 * n, :, st], XS, None, ALU.mult))
                        last = TT(vec[:, l, 2, n, st, :], mod[:, 3 * n + 2, :, st], sm(l, "g_post", KD * n, KD), ALU.mult)
                        if (l, n, st) == (LAYERS - 1, 1, 1):
                            last.then_inc(S["vec_ready"], 1)
            dve.wait_ge(S["vec_ready"], 1)
            inverse_root(0, 0)

            for l in range(LAYERS):
                t0 = first_tok(l)
                sp0 = spans(t0)
                u0 = unit0(l, "in")
                scale_rows(l, 0, 0)
                for i in range(CD_UNITS):
                    lo_part(u0 + i + 1, (i + 1) % 2, KD)
                dve.wait_ge(S["slot_free"], u0 + 6)
                for j in range(2):
                    for p0, c0, n in segs(l):
                        last = STT(Xpad[:, j, p0:p0 + n], Gpad[:, j, p0:p0 + n], 1.0, Xpad[:, j, p0:p0 + n],
                                   ALU.add, ALU.mult)
                    last.then_inc(S["glu"], 1)
                dve.wait_ge(S["glu"], at("glu", l) + 2)
                dve.wait_ge(S["pads_zero"], at("pads_zero", l) + 1)
                lanes = [(j, sg) for j in range(2) for sg in segs(l)]
                NL = len(lanes)

                def tap(n):
                    for x, (j, (p0, c0, w)) in enumerate(lanes):
                        acc = R[:, Y + 6 + j, c0:c0 + w]
                        wv = small[:, l, bass.ds(SM_AT["conv_w"][0] + j * TAPS + n, 1)]
                        src = Xpad[:, j, bass.ds(p0 - HALF + n, w)]
                        if isinstance(n, int) and n == 0:
                            TS(acc, src, wv, sm(l, "conv_b", j), ALU.mult, ALU.add).then_inc(S["conv"], 1)
                        else:
                            dve.wait_ge(S["conv"], at("conv", l) + NL * n + (x + 1 - NL))
                            STT(acc, src, wv, acc, ALU.mult, ALU.add).then_inc(S["conv"], 1)

                tap(0)

                def b_step(first_tap, gate, row0):
                    def f(i, j, r):
                        for x in range(3):
                            tap(3 * i + (first_tap + x))
                        if gate:
                            dve.wait_ge(S["gate_tanh"], at("gate_tanh", l) + i + 1)
                            row = R[:, bass.ds(G + 6 + i, 1), t0:]
                            STT(row, row, 1.0, slot(j, t0).rearrange("p (a t) -> p a t", a=1),
                                ALU.add, ALU.mult).then_inc(S["slot_free"], 1)
                    return f

                units(u0 + 6, 4, b_step(1, False, 0))
                units(u0 + 10, 2, b_step(13, False, 0))
                units(u0 + 12, 4, b_step(19, True, 0))
                for j in range(2):
                    for c, (c0, c1) in enumerate(sp0):
                        n = j * len(sp0) + c
                        dve.wait_ge(S["pool_hi"], at("pool_hi", l) + n + 1)
                        STT(hl(Y + 4 + j, 1, c0, c1), PS[:, 6 + n % 2, 0:c1 - c0], sm(l, "s_pool", j),
                            hl(Y + 4 + j, 0, c0, c1), ALU.mult, ALU.subtract).then_inc(S["pool_done"], 1)
                dve.wait_ge(S["mean_ps"], at("mean_ps", l) + 1)
                for j in range(2):
                    acc = R[:, Y + 6 + j, t0:]
                    STT(acc, slot(0, t0), -1.0 / 256, acc, ALU.mult, ALU.add).then_inc(S["centered"], 1)
                dve.wait_ge(S["ln_root"], at("ln_root", l) + 1)
                dve.wait_ge(S["centered"], at("centered", l) + 2)
                own.link(nc.vector.reciprocal(xrow(2)[:, t0:], xrow(2)[:, t0:]))
                for j in range(2):
                    acc = R[:, Y + 6 + j, t0:]
                    own.link(TT(acc, acc, xrow(2)[:, t0:], ALU.mult))
                    TS(acc, acc, sm(l, "ln_g", j), sm(l, "ln_b", j), ALU.mult, ALU.add).then_inc(S["zed"], 1)
                for j in range(2):
                    dve.wait_ge(S["zed_tanh"], at("zed_tanh", l) + j + 1)
                    STT(xrow(j)[:, t0:], xrow(j)[:, t0:], 1.0, R[:, Y + 6 + j, t0:],
                        ALU.add, ALU.mult).then_inc(S["silu"], 1)
                for e in range(2):
                    for c, (c0, c1) in enumerate(sp0):
                        n = e * len(sp0) + c
                        dve.wait_ge(S["pw_hi"], at("pw_hi", l) + n + 1)
                        STT(hl(Y + 6 + e, 1, c0, c1), PS[:, 6 + n % 2, 0:c1 - c0], XS * 0.5,
                            hl(Y + 6 + e, 0, c0, c1), ALU.mult, ALU.subtract).then_inc(S["pw_done"], 1)

                dve.wait_ge(S["b_tab"], at("b_tab", l) + 32)
                for i, row in enumerate((G, G + 1, G + 4, G + 5)):
                    tr = 0 if i < 2 else t0
                    dve.wait_ge(S["roped_ps"], at("roped_ps", l) + i + 1)
                    ch = [(c, min(c + 640, TOK)) for c in range(tr, TOK, 640)]
                    for x, (c0, c1) in enumerate(ch):
                        TT(T[:, 0:c1 - c0], slot(i % 2, tr)[:, c0 - tr:c1 - tr], xrow(3)[:, c0:c1], ALU.mult)
                        own.link(TT(R[:, row, c0:c1], R[:, row, c0:c1], xrow(2)[:, c0:c1], ALU.mult))
                        last = TT(R[:, row, c0:c1], R[:, row, c0:c1], T[:, 0:c1 - c0], ALU.add)
                        if x == len(ch) - 1:
                            last.then_inc(S["roped"], 1)
                        else:
                            own.link(last)
                    dve.wait_ge(S["roped"], at("roped", l) + i + 1)

                def by_head(col0, half):
                    return rtab[:, col0 + 4 * half:col0 + 4 * half + 4].rearrange("p (h e) -> p h e", e=1).to_broadcast([P, HB, 64])

                heads = lambda ap: ap.rearrange("p (h e) -> p h e", h=HB)

                dve.memset(Sb[:, B_ORDER[0], :], 0.0).then_inc(S["state"], 1)
                for i in range(NTILE - 1):
                    t, nx = B_ORDER[i], B_ORDER[i + 1]
                    dve.wait_ge(S["v_tok"], at("v_tok", l) + i + 1)
                    if i >= 2:
                        dve.wait_ge(S["kv_ps"], at("kv_ps", l) + i - 1)
                    TT(heads(T[:, 512 + (i % 2) * 256:768 + (i % 2) * 256]), heads(vtok[:, t, :]), by_head(8, 1),
                       ALU.mult).then_inc(S["vw"], 1)
                    dve.wait_ge(S["kv_ps"], at("kv_ps", l) + i + 1)
                    dve.wait_ge(S["state"], at("state", l) + i + 1)
                    own.link(TT(Sb[:, nx, :].rearrange("p (q e) -> p q e", q=2),
                                PS[:, 7, 0:256].rearrange("p (q e) -> p q e", q=2),
                                blockm[:, :].rearrange("p (q e) -> p q e", q=1).to_broadcast([P, 2, P]), ALU.mult))
                    for q in range(2):
                        last = STT(Sb[:, nx, q * P:(q + 1) * P], Sb[:, t, q * P:(q + 1) * P], g128[:, q:q + 1],
                                   Sb[:, nx, q * P:(q + 1) * P], ALU.mult, ALU.add)
                    last.then_inc(S["state"], 1)
                tq = t0 // P
                Sf = lambda t: T[:, 512 + (t % 2) * 256:768 + (t % 2) * 256]
                dve.memset(Sf(0), 0.0).then_inc(S["state2"], 1)
                dve.wait_ge(S["d_tab"], at("d_tab", l) + 16)
                dve.wait_ge(S["k_tok"], at("k_tok", l) + NTILE)
                for t in range(NTILE):
                    if t < NTILE - 1:
                        if t:
                            dve.wait_ge(S["kv2_ps"], at("kv2_ps", l) + t)
                        TT(heads(T[:, 256:512]), heads(vtok[:, t, :]), by_head(8, 0), ALU.mult).then_inc(S["vw2"], 1)
                    n = t - tq
                    if n >= 0:
                        dve.wait_ge(S["sc_ps"], at("sc_ps", l) + n + 1)
                        if n:
                            dve.wait_ge(S["y_ps"], at("y_ps", l) + n)
                        for dr in range(2):
                            for x in range(2):
                                last = TT(pmask[:, dr, x:HB:2, :], PS[:, 4 * x, 0:256].rearrange("p (h c) -> p h c", h=2),
                                          dmask[:, dr, x:HB:2, :], ALU.mult)
                        last.then_inc(S["masked"], 1)
                    if t < NTILE - 1:
                        dve.wait_ge(S["kv2_ps"], at("kv2_ps", l) + t + 1)
                        dve.wait_ge(S["state2"], at("state2", l) + t + 1)
                        if n > 0:
                            dve.wait_ge(S["y_ps"], at("y_ps", l) + n)
                        own.link(TT(Sf(t + 1).rearrange("p (q e) -> p q e", q=2),
                                    PS[:, 7, 0:256].rearrange("p (q e) -> p q e", q=2),
                                    blockm[:, :].rearrange("p (q e) -> p q e", q=1).to_broadcast([P, 2, P]), ALU.mult))
                        for q in range(2):
                            last = STT(Sf(t + 1)[:, q * P:(q + 1) * P], Sf(t)[:, q * P:(q + 1) * P], g128[:, q:q + 1],
                                       Sf(t + 1)[:, q * P:(q + 1) * P], ALU.mult, ALU.add)
                        last.then_inc(S["state2"], 1)
                    if n < 0:
                        continue
                    y8 = ysum.rearrange("p (g e) -> p g e", g=8)
                    s8 = SW[:, 0:512].rearrange("p (g e) -> p g e", g=8)
                    b8 = lambda ap: ap.rearrange("p (g e) -> p g e", e=1).to_broadcast([P, 8, 64])
                    dve.wait_ge(S["y_ps"], at("y_ps", l) + n + 1)
                    if n:
                        dve.wait_ge(S["yb_done"], at("yb_done", l) + n)
                    own.link(TT(s8, PS[:, 2, :].rearrange("p (g e) -> p g e", g=8), b8(cross), ALU.mult))
                    own.link(TT(ysum, PS[:, 1, :], SW[:, 0:512], ALU.add))
                    own.link(RED(st8[:, 0, :], y8, AX.X, ALU.add))
                    own.link(TS(st8[:, 1, :], st8[:, 0, :], 1.0 / 64, None, ALU.mult))
                    TT(y8, y8, b8(st8[:, 1, :]), ALU.subtract).then_inc(S["y_mid"], 1)
                    dve.wait_ge(S["y_sq"], at("y_sq", l) + n + 1)
                    own.link(RED(st8[:, 2, :], s8, AX.X, ALU.add))
                    TS(st8[:, 3, :], st8[:, 2, :], 1.0 / 64, 1e-6, ALU.mult, ALU.add).then_inc(S["y_var"], 1)
                    dve.wait_ge(S["y_pow"], at("y_pow", l) + n + 1)
                    TT(y8, y8, b8(st8[:, 0, :]), ALU.mult).then_inc(S["y_norm"], 1)
                    dve.wait_ge(S["yt_ps"], at("yt_ps", l) + n + 1)
                    for dr in range(2):
                        last = TT(SW[:, dr * 256:(dr + 1) * 256].rearrange("p (j t) -> p j t", j=2),
                                  PS[:, 3, dr * 256:(dr + 1) * 256].rearrange("p (j t) -> p j t", j=2),
                                  R[:, G + 6 + 2 * dr:G + 8 + 2 * dr, t * P:(t + 1) * P], ALU.mult)
                    own.link(last)
                    TT(SW[:, 0:256], SW[:, 0:256], SW[:, 256:512], ALU.add).then_inc(S["yb_sum"], 1)
                    dve.wait_ge(S["yb_hi"], at("yb_hi", l) + n + 1)
                    STT(hlr(Y + 2, 2, 1, t * P, P), SW[:, 0:256].rearrange("p (j t) -> p j t", j=2), XS * 0.5 * UNS,
                        hlr(Y + 2, 2, 0, t * P, P), ALU.mult, ALU.subtract).then_inc(S["yb_done"], 1)

                tr = [0, 0, t0, t0]

                def rotate(i):
                    ch = spans(tr[i])
                    done = sum(len(spans(tr[x])) for x in range(i))
                    row = R[:, Y + i % 2, :]

                    def turn(c):
                        c0, c1 = ch[c]
                        w = c1 - c0
                        dve.wait_ge(S["perm_ps"], at("perm_ps", l) + done + c + 1)
                        TT(T[:, 0:w], PS[:, 6, 0:w], xrow(3)[:, c0:c1], ALU.mult)
                        own.link(TT(row[:, c0:c1], row[:, c0:c1], xrow(2)[:, c0:c1], ALU.mult))
                        if done + c:
                            dve.wait_ge(S["rot_lo"], at("rot_lo", l) + done + c)
                        TT(T[:, 512:512 + w], row[:, c0:c1], T[:, 0:w], ALU.add).then_inc(S["rot"], 1)
                        dve.wait_ge(S["rot_hi"], at("rot_hi", l) + done + c + 1)
                        TT(hl(Y + i % 2, 0, 2 * c0 + w, 2 * c0 + 2 * w), T[:, 512:512 + w],
                           hl(Y + i % 2, 0, 2 * c0, 2 * c0 + w), ALU.subtract).then_inc(S["rot_lo"], 1)
                    for c in range(len(ch)):
                        turn(c)

                dve.wait_ge(S["a_tab"], at("a_tab", l) + 64)
                for i in range(A_UNITS):
                    lo_part(u0 + 16 + i + 1, (i + 1) % 2, KD)
                    if 1 <= i <= 4:
                        rotate(i - 1)
                for t in range(NTILE):
                    dve.wait_ge(S["vt_hi"], at("vt_hi", l) + t + 1)
                    TT(Vst[:, t, :, 1, :], PS[:, 6 + t % 2, 0:256].rearrange("p (h e) -> p h e", h=HA),
                       Vst[:, t, :, 0, :], ALU.subtract).then_inc(S["vt_done"], 1)
                for run, t_first, nt, nk in attend_runs(l):
                    attend(l, run, t_first, nt, nk)

                units(unit0(l, "out"), KD, lambda i, j, r: None)
                inverse_root(4 * l + 1, t0)
                add_to_h(l, 0, U, t0)
                inverse_root(4 * l + 2, t0)
                scale_rows(l, 1, t0)

                done = 0
                for q, nf in enumerate(FPARTS):
                    def ffn_evac(i, j, r):
                        if j == 0:
                            dve.wait_ge(S["g_tanh"], at("g_tanh", l) + r + (done + 1))
                            STT(xrow(2)[:, t0:], xrow(1)[:, t0:], 1.0, slot(0, t0), ALU.add, ALU.mult).then_inc(S["slot_free"], 1)
                        else:
                            dve.wait_ge(S["units"], i + (unit0(l, "gu", q) + 1))
                            dve.wait_ge(S["slot_free"], i + unit0(l, "gu", q))
                            STT(xrow(3)[:, t0:], xrow(2)[:, t0:], 2.0 ** -17, slot(1, t0), ALU.mult, ALU.mult).then_inc(S["slot_free"], 1)
                            dve.wait_ge(S["ffn_hi"], at("ffn_hi", l) + r + (done + 1))
                            TT(R16[:, bass.ds(G + r, 1), TOK + t0:2 * TOK], xrow(3)[:, t0:].rearrange("p (a t) -> p a t", a=1),
                               R16[:, bass.ds(G + r, 1), t0:TOK], ALU.subtract).then_inc(S["ffn_lo"], 1)

                    def down_evac(i, j, r):
                        if q:
                            dve.wait_ge(S["units"], i + (unit0(l, "down", q) + 1))
                            row = R[:, bass.ds(Y + i, 1), t0:]
                            STT(row, slot(j, t0).rearrange("p (a t) -> p a t", a=1), UNS, row,
                                ALU.mult, ALU.add).then_inc(S["slot_free"], 1)

                    units(unit0(l, "gu", q), 2 * nf, ffn_evac)
                    units(unit0(l, "down", q), KD, down_evac)
                    done += nf
                inverse_root(4 * l + 3, t0)
                add_to_h(l, 1, Y, t0)
                if l < LAYERS - 1:
                    inverse_root(4 * l + 4, t0)

        @block.gpsimd
        def _(pool):
            TT = nc.gpsimd.tensor_tensor
            own = Chain(pool, S["pool_own"])

            def add_squares(inst, t0):
                for d in range(KD):
                    q = KD * inst + d
                    pool.wait_ge(S["sq_ready"], q + 1)
                    if d == 0:
                        if inst:
                            pool.wait_ge(S["sumsq"], inst)
                        nc.gpsimd.tensor_copy(xrow(0)[:, t0:], xrow(2)[:, t0:]).then_inc(S["sq_used"], 1)
                    else:
                        pool.wait_ge(S["sq_used"], q)
                        TT(xrow(0)[:, t0:], xrow(0)[:, t0:], xrow(2 + d % 2)[:, t0:], ALU.add).then_inc(S["sq_used"], 1)

            pool.memset(nhalf[:, :], -0.5).then_inc(S["small_const"], 1)
            pool.memset(epsv[:, 0:1], 1e-6).then_inc(S["small_const"], 1)
            pool.memset(epsv[:, 1:2], 1e-5).then_inc(S["small_const"], 1)
            pool.memset(beta[:, :], 0.0)
            add_squares(0, 0)

            for l in range(LAYERS):
                t0 = first_tok(l)
                u0 = unit0(l, "in")
                pool.wait_ge(S["u_done"], 2 * KD * l + KD)
                if l:
                    pool.wait_ge(S["slot_free"], u0)
                gaps = [(0, HALF), (HALF + CTX, HALF), (PADW - HALF, HALF)] if not t0 else \
                    [(0, 2 * HALF + CTX), (PADW - HALF, HALF)]
                for g0, n in gaps:
                    pool.memset(Gpad[:, 2:4, g0:g0 + n], 0.0)
                    last = pool.memset(Xpad[:, 0:2, g0:g0 + n], 0.0)
                last.then_inc(S["pads_zero"], 1)
                pool.wait_ge(S["pads_zero"], at("pads_zero", l) + 1)
                pool.wait_ge(S["cd_tab"], at("cd_tab", l) + 64)
                for j in range(2):
                    pool.wait_ge(S["slot_free"], u0 + 1 + j)
                    src = Gpad[:, 2 + j, :]
                    a_, b_ = Gpad[:, 4, :], Gpad[:, 5, :]
                    own.link(TT(a_[:, 1:PADW], src[:, 0:PADW - 1], src[:, 1:PADW], ALU.add))
                    own.link(TT(b_[:, 2:PADW - 1], a_[:, 1:PADW - 2], a_[:, 3:PADW], ALU.add))
                    if j:
                        own.link(TT(a_[:, 4:PADW - 3], b_[:, 2:PADW - 5], b_[:, 6:PADW - 1], ALU.add))
                        own.link(TT(b_[:, 8:PADW - 7], a_[:, 4:PADW - 11], a_[:, 12:PADW - 3], ALU.add))
                    for half, w in ((0, a_), (64, b_)):
                        for p0, c0, n in segs(l):
                            last = TT(R[half:half + 64, Y + 2 + j, c0:c0 + n], w[half:half + 64, p0:p0 + n],
                                      R[half:half + 64, Y + j, c0:c0 + n], ALU.mult)
                    own.link(last)
                    for p0, c0, n in segs(l):
                        last = TT(R[:, Y + 2 + j, c0:c0 + n], R[:, Y + 2 + j, c0:c0 + n], src[:, p0:p0 + n], ALU.subtract)
                    last.then_inc(S["pooled"], 1)
                    pool.wait_ge(S["pooled"], at("pooled", l) + j + 1)
                for n in range(NTILE - t0 // P):
                    pool.wait_ge(S["y_var"], at("y_var", l) + n + 1)
                    TT(st8[:, 0, :], st8[:, 3, :], nhalf[:, 0:1].to_broadcast([P, 8]), ALU.pow).then_inc(S["y_pow"], 1)
                for run, t_first, nt, nk in attend_runs(l):
                    with pool.Fori(0, nt) as r:
                        pool.wait_ge(S[f"o_var_{run}{l}"], r + 1)
                        TT(st8[:, 2, 0:4], st8[:, 1, 0:4], nhalf[:, 0:1].to_broadcast([P, 4]),
                           ALU.pow).then_inc(S[f"o_pow_{run}{l}"], 1)
                for inst in range(4 * l + 1, 4 * l + (5 if l < LAYERS - 1 else 4)):
                    add_squares(inst, t0)



def _tables():
    f = np.float32
    tok = np.arange(LAT)
    row, col = (tok // 64).astype(f), (tok % 64).astype(f)

    def rope(d):
        nf = d // 4
        inv = (f(10000.0) ** (-np.arange(nf, dtype=f) / f(nf))).astype(f)
        ang = np.concatenate([row[:, None] * inv, col[:, None] * inv], axis=-1).astype(f)
        c, s = np.cos(ang).T.astype(f), np.sin(ang).T.astype(f)
        C, Sn = np.ones((P, TOK), f), np.zeros((P, TOK), f)
        C[:, CTX:] = np.tile(np.concatenate([c, c]), (P // d, 1))
        Sn[:, CTX:] = np.tile(np.concatenate([-s, s]), (P // d, 1))
        perm = np.zeros((P, P), f)
        for m in range(P):
            perm[m - m % d + (m % d + d // 2) % d, m] = 1
        return np.stack([C, Sn]), perm

    ropeA, permA = rope(DQ)
    ropeB, permB = rope(DK)
    stk = np.zeros((P, 4, 352), np.float16)
    for j in range(4):
        for b in (0, 1, 4, 5, 6, 8, 10):
            for d in range(32):
                stk[32 * j + d, j, 32 * b + d] = 1
    gam = np.exp(np.array(LOG_GAMMA))
    i = np.arange(P)
    dist = i[None, :] - i[:, None]
    dmask = np.zeros((P, 2, HB, P))
    rtab = np.zeros((P, 18))
    for h in range(HB):
        pw = gam[h] ** np.abs(dist) * DK ** -0.5
        dmask[:, 0, h] = np.where(dist >= 0, pw, 0)
        dmask[:, 1, h] = np.where(dist <= 0, pw, 0)
        rtab[:, h] = gam[h] ** (i + 1)
        rtab[:, 4 + h] = gam[h] ** (P - i)
        rtab[:, 8 + h] = gam[h] ** (P - 1 - i) * DK ** -0.5
        rtab[:, 12 + h] = gam[h] ** i * DK ** -0.5
        rtab[64 * (h % 2):64 * (h % 2) + 64, 16 + h // 2] = gam[h] ** P
    cnt = np.zeros((2, P, TOK))
    for g, w in enumerate((2, 4, 8, 16)):
        for n, c0 in ((CTX, 0), (LAT, CTX)):
            pos = np.arange(n)
            k = np.clip(pos + w - w // 2, 0, n) - np.clip(pos - w // 2, 0, n)
            cnt[g // 2, 64 * (g % 2):64 * (g % 2) + 64, c0:c0 + n] = 1.0 / k
    blockm = np.kron(np.eye(2), np.ones((64, 64)))
    return {"ident": np.eye(P, dtype=f), "ones": np.ones((P, P), f), "blockm": blockm.astype(f), "rtab": rtab.astype(f),
            "ropeA": ropeA, "ropeB": ropeB, "permA": permA, "permB": permB, "stk": stk.reshape(P, -1).view(f),
            "dmask": dmask.astype(f).reshape(P, -1), "cnt": cnt.astype(f)}


def _units(w, order=None):
    L, k, n = w.shape
    u = w.reshape(L, k // P, P, n // P, P).transpose(0, 3, 2, 1, 4)
    return np.ascontiguousarray(u if order is None else u[:, order])


def _cols(v):
    return v.reshape(v.shape[0], -1, P).transpose(2, 0, 1)


def layout(i):
    L = LAYERS
    arr = _tables()
    tokens = np.concatenate([i["ctx"][0], i["x"][0]])
    arr["x"] = np.ascontiguousarray(tokens.T.reshape(KD, P, TOK))
    arr["c2"] = np.ascontiguousarray(np.stack([i["c"][0], i["c_ctx"]], -1).reshape(KD, P, 2).transpose(1, 0, 2))
    lam = np.stack([i["lam_q1"], i["lam_k1"], i["lam_q2"], i["lam_k2"]], 1).reshape(1, -1)
    arr["lam"] = np.ascontiguousarray(np.broadcast_to(lam, (P, lam.size)))
    arr["w_ada"] = _units(i["w_ada"]).reshape(L * 48, P, KD, P)
    arr["w_in"] = _units(i["w_in"], [16, 17, 20, 21, 18, 19, 4, 5, 6, 7, 10, 11, 12, 13, 14, 15, 0, 1, 8, 9, 2, 3])
    arr["w_out"] = _units(i["w_out"])
    g, u = _units(i["w_ffn_gate"]), _units(i["w_ffn_up"])
    arr["w_gu"] = np.ascontiguousarray(np.stack([g, u], 2).reshape(L, 2 * NF, P, KD, P))
    f0 = 0
    for q, nf in enumerate(FPARTS):
        arr[f"w_down{q}"] = _units(i["w_ffn_down"][:, f0 * P:(f0 + nf) * P])
        f0 += nf
    pw = i["w_conv_out"].reshape(L, 2, P, 256).transpose(0, 2, 1, 3).reshape(L, P, 512)
    wp = np.zeros((L, P, 2, P), np.float32)
    for gi in range(4):
        o = 64 * (gi % 2)
        wp[:, o:o + 64, gi // 2, o:o + 64] = i["w_pool"][:, gi]
    arr["swb"] = np.ascontiguousarray(np.concatenate([pw, wp.reshape(L, P, 256)], -1))
    sub = np.broadcast_to(i["g_subln"][:, None, :], (L, 2, DV)).reshape(L, P)
    cw = i["conv_w"][:, :, 0, :].reshape(L, TAPS, 2, P).transpose(3, 0, 2, 1).reshape(P, L, 2 * TAPS)
    parts = [np.concatenate([_cols(i["g_pre_mix"]), _cols(i["g_pre_ffn"])], -1),
             np.concatenate([_cols(i["g_post_mix"]), _cols(i["g_post_ffn"])], -1),
             cw, _cols(i["conv_b"]), _cols(i["conv_ln_g"]), _cols(i["conv_ln_b"]), _cols(i["s_pool"]), _cols(sub)]
    arr["b_ada"] = np.ascontiguousarray(_cols(i["b_ada"]).reshape(P, -1))
    arr["small"] = np.ascontiguousarray(np.concatenate(parts, -1))
    return arr


def kernel(**inputs):
    import concourse.bacc as _bacc
    from concourse.bass_utils import run_bass_kernel_spmd as _run

    arrays = layout({k: np.asarray(v) for k, v in inputs.items()})
    nc = _bacc.Bacc("TRN2", target_bir_lowering=False, num_devices=1)
    aps = {k: nc.dram_tensor("in_" + k, v.shape, mybir.dt.from_np(v.dtype), kind="ExternalInput").ap() for k, v in arrays.items()}
    out = nc.dram_tensor("out", (KD, P, LAT), F32, kind="ExternalOutput").ap()
    build(nc, aps, out)
    r = _run(nc, [{"in_" + k: v for k, v in arrays.items()}], core_ids=[0])
    got = r.results[0]["out"]
    return np.ascontiguousarray(got.reshape(1, D, LAT).transpose(0, 2, 1))
```

```python
import math
from contextlib import ExitStack

import numpy as np

import concourse.bass as bass
from concourse import mybir

ALU = mybir.AluOpType
ACT = mybir.ActivationFunctionType
AX = mybir.AxisListType
F32 = mybir.dt.float32
F16 = mybir.dt.float16

P = 128
D = 1024
KD = D // P
LAYERS = 2
CTX, LAT = 256, 1024
TOK = CTX + LAT
NTILE = TOK // P
CT = CTX // P
DFF = 2816
NF = DFF // P
FPARTS = (8, 8, 6)
NIN = 22
HA, DQ, DV = 4, 32, 64
HB, DK = 4, 64
TAPS, HALF = 31, 15
PADW = HALF + CTX + HALF + LAT + HALF
SEG = ((HALF, 0, CTX), (2 * HALF + CTX, CTX, LAT))
WS, XS = 64.0, 16.0
UNS = 1.0 / (WS * XS)
H, U, G, Y = 0, 8, 16, 24
CD_UNITS, B_UNITS, A_UNITS = 6, 10, 6
LAYER_UNITS = NIN + KD + 2 * NF + KD * len(FPARTS)
LAM_INIT = [0.8 - 0.6 * math.exp(-0.3 * l) for l in range(LAYERS)]
LOG_GAMMA = [math.log(1.0 - 2.0 ** (-5 - h)) for h in range(HB)]
SCORE = DQ ** -0.5 / (XS * XS)
SMALLS = {"g_pre": KD * 2, "g_post": KD * 2, "conv_w": 2 * TAPS, "conv_b": 2, "ln_g": 2, "ln_b": 2,
          "s_pool": 2, "g_sub": 1}
SM_AT = {}
_at = 0
for _k, _n in SMALLS.items():
    SM_AT[_k] = (_at, _n)
    _at += _n
SM_W = _at


def spans(t0):
    return [(a, min(a + 512, TOK)) for a in range(t0, TOK, 512)]


class Chain:

    def __init__(self, eng, s):
        self.eng, self.s, self.base, self.k = eng, s, 0, 0

    def link(self, ins):
        ins.then_inc(self.s, 1)
        self.k += 1
        self.eng.wait_ge(self.s, self.base + self.k)

    def enter(self, r, per):
        self.outer = self.base + self.k
        self.base, self.k = self.outer + r * per, 0

    def leave(self, n, per):
        assert self.k == per, (self.k, per)
        self.base, self.k = self.outer + n * per, 0


def build(nc, a, out):
    with ExitStack() as ctx:
        def sb(name, shape, dt=F32):
            return ctx.enter_context(nc.sbuf_tensor(name, shape, dt))

        def sem(name):
            return ctx.enter_context(nc.semaphore(name))

        R = sb("R", [P, 32, TOK])
        X = sb("X", [P, 4 * PADW])
        stage = sb("stage", [P, 2, KD, P])
        whi = sb("whi", [P, 2, KD, P], F16)
        wlo = sb("wlo", [P, 2, KD, P], F16)
        ident = sb("ident", [P, P])
        ones = sb("ones", [P, P])
        perm = sb("perm", [P, P])
        SW = sb("SW", [P, 768])
        T = sb("T", [P, 1024])
        small = sb("small", [P, LAYERS, SM_W])
        vec = sb("vec", [P, LAYERS, 3, 2, 2, KD])
        csil = sb("csil", [P, KD, 2])
        bada = sb("bada", [P, 48])
        tiny = sb("tiny", [P, 44])
        lamv = tiny[:, 8:24]
        rtab = tiny[:, 26:44]
        nhalf = tiny[:, 0:1]
        epsv = tiny[:, 1:3]
        smax = tiny[:, 4:8].rearrange("p (b c) -> p b c", b=2)
        nbias = tiny[:, 8:12].rearrange("p (b c) -> p b c", b=2)
        den = tiny[:, 12:16].rearrange("p (b c) -> p b c", b=2)
        beta = tiny[:, 24:26]
        st8 = sb("st8", [P, 4, 8])
        rl, rinv = st8[:, 3, 0:4], st8[:, 3, 4:8]
        PS = ctx.enter_context(nc.psum_tensor("PS", [P, 8, 512], F32))

        R16 = R[:, :, :].rearrange("p r t -> p (r t)").bitcast(F16).rearrange("p (r t) -> p r t", r=32)
        PSF = PS[:, :, :].rearrange("p b t -> p (b t)")

        def hl(row, part, c0, c1):
            return R16[:, row, part * TOK + c0:part * TOK + c1]

        def hlr(row, n, part, c0, w):
            return R16[:, row:row + n, bass.ds(part * TOK + c0, w)]

        def slot(s, t0=0):
            return PSF[:, 1536 * s:1536 * s + TOK - t0]

        def sm(l, k, i=0, n=1):
            at = SM_AT[k][0] + i
            return small[:, l, at:at + n]

        def vv(l, kind, norm, stream, d):
            return vec[:, l, kind, norm, stream, d:d + 1]

        def xrow(i):
            return X[:, i * PADW:i * PADW + TOK]

        Xpad = X[:, :].rearrange("p (r t) -> p r t", r=4)
        Gpad = R[:, G:G + 7, :].rearrange("p r t -> p (r t)")[:, 0:6 * PADW].rearrange("p (r t) -> p r t", r=6)
        vtok = X[:, 0:NTILE * 256].rearrange("p (t c) -> p t c", c=256)
        Vst = X[:, 0:NTILE * 256].bitcast(F16).rearrange("p (t h x e) -> p t h x e", t=NTILE, h=HA, x=2)
        wpw = SW[:, 0:512].rearrange("p (k e) -> p k e", k=2)
        wpool = SW[:, 512:768].rearrange("p (k e) -> p k e", k=2)
        stk = SW[:, :].bitcast(F16)[:, 0:4 * 352].rearrange("p (j c) -> p j c", j=4)
        Kst = R16[:, G:G + 4, :].rearrange("p r t -> p (r t)").rearrange("p (h t) -> p h t", h=8)
        Qst = R16[:, G + 4:G + 8, :].rearrange("p r t -> p (r t)").rearrange("p (h t) -> p h t", h=8)
        RB = R[:, 18:20, :].rearrange("p r t -> p (r t)")
        dmask = RB[:, 0:1024].rearrange("p (d h c) -> p d h c", d=2, h=HB)
        pmask = RB[:, 1024:2048].rearrange("p (d h c) -> p d h c", d=2, h=HB)
        ycross = RB[:, 2048:2560]
        ysum = [T[:, 0:512], T[:, 512:1024]]
        Sf, Sb = (X[:, 2 * PADW + dr * NTILE * P:2 * PADW + (dr + 1) * NTILE * P].rearrange("p (t c) -> p t c", c=P)
                  for dr in range(2))
        vw_fwd = SW[:, 0:512]
        KV_BANKS = ((7, 4), (5, 2))
        P1 = [R[:, U + i, :] for i in range(2)]
        P2 = [R[:, U + 2 + i, :] for i in range(2)]
        Wt = [R[:, U + 4 + i, :] for i in range(2)]
        wtb = [R16[:, row, c0:c0 + 2 * w].rearrange("p (x c) -> p x c", x=2)
               for row, c0, w in ((U + 6, 0, 512), (U + 6, 1024, 512), (U + 6, 2048, 256), (U + 7, 1536, 512))]
        AO = R[:, U + 7, 0:768].rearrange("p (i h e) -> p i h e", i=3, h=HA)

        cross = rtab[:, 0:8]
        wend = rtab[:, 8:16]
        g128 = rtab[:, 16:18]

        PER_LAYER = dict(
            cd_tab=64, pads_zero=1, glu=2, conv=TAPS * 4, pooled=2, pool_ps=6, pool_hi=6, pool_done=6,
            mean_ps=1, centered=2, cd_sq=2, var_ps=1, ln_root=1, zed=2, zed_tanh=2, silu=2, pw_ps=6, pw_hi=6, pw_done=6,
            b_tab=32, gate_tanh=4, roped_ps=4, roped=4, d_tab=16,
            states_zero=1, tr_ps=NTILE, v_tok=NTILE, k_tok=NTILE, vw=NTILE, kv_ps=NTILE, state=NTILE - 1, kv_fwd=NTILE - 1,
            state_fwd=NTILE - 1,
            sc_ps=NTILE, masked=NTILE, y_ps=NTILE, y_mid=NTILE, y_sq=NTILE, y_var=NTILE, y_pow=NTILE, y_norm=NTILE,
            yt_ps=NTILE, yb_sum=NTILE, yb_hi=NTILE, yb_done=NTILE,
            a_tab=64, perm_ps=12, rot=12, rot_hi=12, rot_lo=12, stk_ps=48, stk_act=24, stk_dve=24,
            vt_ps=NTILE, vt_hi=NTILE, vt_done=NTILE, g_tanh=NF, ffn_hi=NF, ffn_lo=NF)
        S = {n: sem(n) for n in
             ("consts smalls b_ada csil c_tanh lam_dots lam_exp ada_used vec_ready small_const w_hi w_lo units "
              "slot_free act_own dve_own pool_own h_in out_done sq_ready sq_used sumsq root u_scaled u_hi u_done h_rows").split()}
        S |= {n: sem(n) for n in PER_LAYER}
        ada_landed = [sem(f"ada_landed{i}") for i in range(8)]
        w_landed = [sem(f"w_landed{j}") for j in range(2)]
        ffn_ring_landed = [sem(f"ffn_ring_landed{j}") for j in range(2)]
        ring_landed = [sem(f"ring_landed{j}") for j in range(3)]
        for l in range(LAYERS):
            for run in (("c", "l") if l < LAYERS - 1 else ("l",)):
                for n in "scores nbias exps w wt_ps wt_hi wt_lo pv o_sum o_var o_pow o_norm ot_ps ot_hi ot_done".split():
                    S[f"{n}_{run}{l}"] = sem(f"{n}_{run}_{l}")

        X16 = X[:, :].bitcast(F16)
        STACK_BANKS = (6, 7, 0, 3)
        VALUE_BANKS = (1, 4, 2, 5)

        def arow(i):
            return (R[:, Y + i, :], xrow(i - 2), R[:, U + i - 4, :])[i // 2]

        def arow16(i, c0, c1):
            return R16[:, Y + i, c0:c1] if i < 2 else X16[:, 2 * PADW * (i - 2) + c0:2 * PADW * (i - 2) + c1]

        def rotary(l):
            return [(i, c0, c1) for i in range(4) for c0, c1 in spans(0 if i < 2 else first_tok(l))]

        def stacks(l):
            return [(m, i, j, c0, c1) for m, (i, c0, c1) in enumerate(rotary(l)) for j in range(4)]

        def at(name, l):
            return PER_LAYER[name] * l

        def unit0(l, stage, part=0):
            at = l * LAYER_UNITS
            if stage == "in":
                return at
            at += NIN
            if stage == "out":
                return at
            at += KD
            for q in range(part):
                at += 2 * FPARTS[q] + KD
            return at if stage == "gu" else at + 2 * FPARTS[part]

        def gemm_list():
            out_ = []
            for l in range(LAYERS):
                out_ += [8] * (NIN + KD)
                for f in FPARTS:
                    out_ += [8] * (2 * f) + [f] * KD
            return out_
        UK = gemm_list()
        assert len(UK) == LAYERS * LAYER_UNITS

        def row_lat(l, after_mix=True):
            return CTX if l == LAYERS - 1 else 0

        block = ctx.enter_context(nc.Block())

        B_ORDER = [1, 0] + list(range(NTILE - 1, CT - 1, -1))

        def fwd_products(i):
            return sum(t < NTILE - 1 for t in B_ORDER[:i + 1])

        def first_tok(l):
            return CTX if l == LAYERS - 1 else 0

        def segs(l):
            return SEG[1:] if first_tok(l) else SEG

        def streams(t0):
            return [(0, CTX, TOK)] if t0 else [(1, 0, CTX), (0, CTX, TOK)]

        def attend_runs(l):
            runs = [("l", CT, NTILE - CT, NTILE)]
            return runs if first_tok(l) else [("c", 0, CT, CT)] + runs

        def key_groups(nk):
            return [(g, min(4, nk - g)) for g in range(0, nk, 4)]

        def turned(p, w):
            return PS[:, 6, 0:w] if p < 2 else PSF[:, 1536 + TOK:1536 + TOK + w]

        def WTb(h, p):
            return wtb[3] if p == 0 and h % 2 else wtb[p]

        def back(r, h, n):
            return (r, h - n) if h >= n else (r - 1, HA + h - n)

        ADA_FIRST = 2 * KD
        ADA_PER = (3, 4)
        ADA_FFN = 3 * KD
        ADA_SLOTS = (3, 2)
        ADA_COL = 7 * 512 + HA * DV
        ADA_STEPS = ({(0, 0): (0,), (1, 0): (1,), (3, 0): (2,)},
                     {(0, 0): (0,), (1, 0): (1,), (2, 1): (2,), (3, 0): (3,)})
        ring = [X[:, 2560:3584], X[:, 3584:4608], T[:, :]]

        def ada0(l):
            return ADA_FIRST + l * (ADA_PER[0] * (LAT // P) + ADA_FFN)

        ADA_F0 = ada0(1) - ADA_FFN
        ffn_ring = [T[:, :], X[:, 0:1024]]

        def pairs(eng, n, body, start=0):
            for i in range(2 * start):
                body(i, i, 0)
            if n > 2 * start + 2:
                with eng.Fori(start, n // 2 - 1) as r:
                    for j in range(2):
                        body(2 * r + j, j, r)
            for j in range(2):
                body(n - 2 + j, j, n // 2 - 1)

        @block.sync
        def _(sp):
            sp.dma_start(small[:, :, :], a["small"]).then_inc(S["smalls"], 16)
            sp.dma_start(csil[:, :, :], a["c2"]).then_inc(S["smalls"], 16)
            sp.dma_start(T[:, 0:256], a["lam"]).then_inc(S["smalls"], 16)
            sp.dma_start(bada[:, 0:ADA_FIRST], a["b_ada"][:, 0:ADA_FIRST]).then_inc(S["b_ada"], 16)
            sp.dma_start(ones[:, :], a["ones"]).then_inc(S["smalls"], 16)
            for d in range(KD):
                sp.dma_start(R[:, H + d, :], a["x"][d]).then_inc(S["h_in"], 16)
            for i in range(ADA_FIRST):
                sp.dma_start(R[:, G + i, 0:1024].rearrange("p (k m) -> p k m", k=KD), a["w_ada"][i]
                             ).then_inc(ada_landed[i % 8], 16)
            for name, dst in (("ident", ident), ("rtab", rtab)):
                sp.dma_start(dst[:, :], a[name]).then_inc(S["consts"], 16)

            def modulation(i, j):
                sp.wait_ge(S["ada_used"], i + (ADA_F0 - 1))
                sp.dma_start(ffn_ring[j].rearrange("p (k m) -> p k m", k=KD),
                             a["w_ada"][bass.ds(i + ADA_F0, 1)].rearrange("a p k m -> p (a k) m")
                             ).then_inc(ffn_ring_landed[j], 16)

            def stream(u0, n, K, src, then=None):
                start = 0
                if u0 == 0:
                    for j in range(2):
                        sp.dma_start(stage[:, j, 0:K, :], src[j]).then_inc(w_landed[j], 16)
                    start = 1
                if start == n // 2:
                    return
                with sp.Fori(start, n // 2) as r:
                    for j in range(2):
                        sp.wait_ge(S["w_lo"], 2 * r + (u0 + j - 1))
                        sp.dma_start(stage[:, j, 0:K, :], src[bass.ds(2 * r + j, 1)].rearrange("a p k m -> p (a k) m")
                                     ).then_inc(w_landed[j], 16)
                        if then:
                            then(r, j)

            for l in range(LAYERS):
                stream(unit0(l, "in"), 2, KD, a["w_in"][l][0:2])
                if l == 0:
                    sp.wait_ge(S["ada_used"], ADA_FIRST)
                else:
                    sp.wait_ge(S["h_rows"], 2 * KD * l)
                    sp.wait_ge(S["stk_ps"], at("stk_ps", l-1) + 4 * 2 * (len(spans(0)) + len(spans(first_tok(l - 1)))))
                for j in range(2):
                    sp.dma_start(R[:, Y + j, :], a["cnt"][j]).then_inc(S["cd_tab"], 16)
                sp.dma_start(SW[:, :], a["swb"][l]).then_inc(S["cd_tab"], 16)
                sp.dma_start(perm[:, :], a["permB"]).then_inc(S["cd_tab"], 16)
                ahead = CD_UNITS + B_UNITS + 2
                stream(unit0(l, "in") + 2, ahead - 2, KD, a["w_in"][l][2:ahead])
                sp.wait_ge(S["silu"], at("silu", l) + 2)
                for j in range(2):
                    sp.dma_start(xrow(2 + j), a["ropeB"][j]).then_inc(S["b_tab"], 16)
                sp.wait_ge(S["tr_ps"], at("tr_ps", l) + NTILE)
                sp.dma_start(RB[:, 0:1024], a["dmask"]).then_inc(S["d_tab"], 16)
                sp.wait_ge(S["yb_done"], at("yb_done", l) + NTILE - first_tok(l) // P)
                for j in range(2):
                    sp.dma_start(xrow(2 + j), a["ropeA"][j]).then_inc(S["a_tab"], 16)
                sp.dma_start(SW[:, 0:704], a["stk"]).then_inc(S["a_tab"], 16)
                sp.dma_start(perm[:, :], a["permA"]).then_inc(S["a_tab"], 16)
                stream(unit0(l, "in") + ahead, NIN - ahead, KD, a["w_in"][l][ahead:NIN])
                stream(unit0(l, "out"), 2, KD, a["w_out"][l][0:2])
                sp.wait_ge(S["stk_ps"], at("stk_ps", l) + len(stacks(l)))
                sp.wait_ge(S["vec_ready"], 2 * l + 1)
                n_ada = ADA_PER[l] * (LAT // P)
                sp.dma_start(bada[:, 0:n_ada], a["b_ada"][:, ada0(l):ada0(l) + n_ada]).then_inc(S["b_ada"], 16)
                with sp.Fori(0, LAT // P) as r:
                    for i in range(ADA_PER[l]):
                        j = i % ADA_SLOTS[l]
                        sp.wait_ge(S["ada_used"], ADA_PER[l] * r + (ada0(l) + i - ADA_SLOTS[l] + 1))
                        sp.dma_start(ring[j].rearrange("p (k m) -> p k m", k=KD),
                                     a["w_ada"][bass.ds(ADA_PER[l] * r + (ada0(l) + i), 1)].rearrange("a p k m -> p (a k) m")
                                     ).then_inc(ring_landed[j], 16)
                stream(unit0(l, "out") + 2, KD - 2, KD, a["w_out"][l][2:KD])
                f0 = 0
                for q, nf in enumerate(FPARTS):
                    gu, down = a["w_gu"][l][2 * f0:2 * (f0 + nf)], a[f"w_down{q}"][l]
                    if l or q:
                        stream(unit0(l, "gu", q), 2 * nf, KD, gu)
                        stream(unit0(l, "down", q), KD, nf, down)
                    else:
                        stream(unit0(l, "gu", q), 2, KD, gu[0:2])
                        sp.wait_ge(S["sumsq"], 3)
                        sp.wait_ge(S["vec_ready"], 2)
                        sp.dma_start(bada[:, 0:ADA_FFN], a["b_ada"][:, ADA_F0:ADA_F0 + ADA_FFN]).then_inc(S["b_ada"], 16)
                        for j in range(2):
                            modulation(j, j)
                        stream(unit0(l, "gu", q) + 2, 2 * nf - 2, KD, gu[2:2 * nf], lambda r, j: modulation(2 * r + (2 + j), j))
                        stream(unit0(l, "down", q), KD, nf, down, lambda r, j: modulation(2 * r + (2 * nf + j), j))
                    f0 += nf
            for d in range(KD):
                sp.wait_ge(S["h_rows"], 2 * KD * LAYERS - KD + d + 1)
                sp.dma_start(out[d], R[:, H + d, CTX:TOK]).then_inc(S["out_done"], 16)
            sp.wait_ge(S["out_done"], 16 * KD)

        @block.tensor
        def _(pe):
            mm = nc.tensor.matmul

            def gemm_unit(u, j, K, row0, t0):
                pe.wait_ge(S["w_lo"], u + 1)
                if not (isinstance(u, int) and u < 2):
                    pe.wait_ge(S["slot_free"], u - 1)
                for c0, c1 in spans(t0):
                    o = slot(j, t0)[:, c0 - t0:c1 - t0]
                    for k in range(K):
                        for q, (w, part) in enumerate(((whi, 0), (whi, 1), (wlo, 0))):
                            last = mm(o, w[:, j, k, :], hl(row0 + k, part, c0, c1),
                                      start=(k == 0 and q == 0), stop=(k == K - 1 and q == 2))
                last.then_inc(S["units"], 1)

            def gemm(u0, n, K, row0, t0, then=lambda i, j, r: None):
                def body(i, j, r):
                    gemm_unit(i + u0, j, K, row0, t0)
                    then(i, j, r)
                pairs(pe, n, body, start=int(u0 == 0))

            def ffn_modulation(i, j, turn):
                pe.wait_ge(ffn_ring_landed[j], 16 * turn + 16)
                for k in range(KD):
                    last = mm(PSF[:, bass.ds(2 * i + 3072, 2)], ffn_ring[j][:, k * P:(k + 1) * P], csil[:, k, :],
                              start=(k == 0), stop=(k == KD - 1))
                last.then_inc(S["ada_used"], 1)

            def sum_rows(inst, t0):
                pe.wait_ge(S["sq_used"], KD * (inst + 1))
                for c0, c1 in spans(t0):
                    last = mm(slot(0, t0)[:, c0 - t0:c1 - t0], ones[:, :], xrow(0)[:, c0:c1], start=True, stop=True)
                last.then_inc(S["sumsq"], 1)

            def attend(l, run, t_first, nt, nk):
                s = lambda n: S[f"{n}_{run}{l}"]
                groups = key_groups(nk)
                NG, keys = len(groups), nk * P

                def scores(r, h, c):
                    n = 4 * r + h
                    if not (isinstance(r, int) and n == 0):
                        pe.wait_ge(s("exps"), 2 * n + (c - 1))
                    if c and NG == 3 and not (isinstance(r, int) and n < 2):
                        pe.wait_ge(s("wt_lo"), NG * n - NG)
                    for k0 in range(0, keys, 512):
                        k1 = min(k0 + 512, keys)
                        last = mm(slot(c)[:, k0:k1], Qst[:, 2 * h + c, bass.ds((t_first + r) * P, P)],
                                  Kst[:, 2 * h + c, k0:k1], start=True, stop=True)
                    last.then_inc(s("scores"), 1)

                def turn(r, h, p):
                    n = 4 * r + h
                    k0, m = groups[p]
                    if p == 0:
                        pe.wait_ge(s("w"), n + 1)
                    if p == 2:
                        pe.wait_ge(s("exps"), 2 * n + 4 if not (isinstance(r, int) and n == 4 * nt - 1) else 2 * n + 2)
                    elif not (isinstance(r, int) and n == 0 and p == 0):
                        pe.wait_ge(s("wt_lo"), NG * n + p)
                    o = turned(p, m * P)
                    for i in range(m):
                        last = nc.tensor.transpose(o[:, i * P:(i + 1) * P],
                                                   Wt[h % 2][:, (k0 + i) * P:(k0 + i + 1) * P], ident[:, :])
                    last.then_inc(s("wt_ps"), 1)

                def values(r, h, p):
                    n = 4 * r + h
                    k0, m = groups[p]
                    pe.wait_ge(s("wt_lo"), NG * n + (p + 1))
                    if p == 0 and h == 0 and not (isinstance(r, int) and r == 0):
                        pe.wait_ge(s("o_sum"), r)
                    for i in range(m):
                        for q, (x, v) in enumerate(((0, 0), (0, 1), (1, 0))):
                            last = mm(PS[:, 7, h * DV:(h + 1) * DV], WTb(h, p)[:, x, i * P:(i + 1) * P],
                                      Vst[:, k0 + i, h, v, :],
                                      start=(k0 + i == 0 and q == 0), stop=(p == NG - 1 and i == m - 1 and q == 2))
                    last.then_inc(s("pv"), 1)

                def modulation(r, h, place):
                    if run != "l":
                        return
                    for i in ADA_STEPS[l].get((h, place), ()):
                        j = i % ADA_SLOTS[l]
                        pe.wait_ge(ring_landed[j], 16 * (l + 1) * r + (LAT // P * 16 * l + 16 * (i // ADA_SLOTS[l] + 1)))
                        for k in range(KD):
                            last = mm(PSF[:, bass.ds(2 * ADA_PER[l] * r + (ADA_COL + 2 * i), 2)],
                                      ring[j][:, k * P:(k + 1) * P], csil[:, k, :], start=(k == 0), stop=(k == KD - 1))
                        last.then_inc(S["ada_used"], 1)

                def turn_out(r):
                    pe.wait_ge(s("o_norm"), r + 1)
                    pe.wait_ge(s("wt_lo"), NG * (4 * r + 5) if not (isinstance(r, int) and r == nt - 1) else NG * 4 * nt)
                    for j in range(2):
                        last = nc.tensor.transpose(PS[:, 6, j * P:(j + 1) * P],
                                                   AO[:, 2, :, :].rearrange("p h e -> p (h e)")[:, j * P:(j + 1) * P],
                                                   ident[:, :])
                    last.then_inc(s("ot_ps"), 1)

                def tile(r, first=False, last=False):
                    for h in range(HA):
                        two = h >= 2 or not first
                        if two:
                            for p in range(1, NG):
                                turn(*back(r, h, 2), p)
                        modulation(r, h, 0)
                        scores(r, h, 1)
                        if h == 2 and not first:
                            turn_out(r - 1)
                            pe.wait_ge(s("ot_done"), r)
                        if h or not first:
                            turn(*back(r, h, 1), 0)
                        if h < HA - 1 or not last:
                            scores(*((r, h + 1) if h < HA - 1 else (r + 1, 0)), 0)
                        if two:
                            for p in range(NG):
                                values(*back(r, h, 2), p)
                        modulation(r, h, 1)

                scores(0, 0, 0)
                tile(0, first=True)
                if nt > 2:
                    with pe.Fori(1, nt - 1) as r:
                        tile(r)
                tile(nt - 1, last=True)
                for h in (HA - 2, HA - 1):
                    if h == HA - 1:
                        turn(nt - 1, h, 0)
                    for p in range(1, NG):
                        turn(nt - 1, h, p)
                    for p in range(NG):
                        values(nt - 1, h, p)
                turn_out(nt - 1)

            pe.wait_ge(S["smalls"], 64)
            sum_rows(0, 0)
            pe.wait_ge(S["csil"], 1)
            for i in range(ADA_FIRST):
                pe.wait_ge(ada_landed[i % 8], 32)
                for k in range(KD):
                    last = mm(PSF[:, 3072 + 2 * i:3074 + 2 * i], R[:, G + i, k * P:(k + 1) * P],
                              csil[:, k, :], start=(k == 0), stop=(k == KD - 1))
                last.then_inc(S["ada_used"], 1)
            pe.wait_ge(S["consts"], 32)

            for l in range(LAYERS):
                t0 = first_tok(l)
                sp0 = spans(t0)
                u0 = unit0(l, "in")
                pe.wait_ge(S["u_done"], 2 * KD * l + KD)
                pe.wait_ge(S["root"], 4 * l + 1)
                gemm(u0, CD_UNITS, KD, U, t0)
                gemm(u0 + 6, 4, KD, U, 0)
                gemm(u0 + 10, 6, KD, U, t0)
                pe.wait_ge(S["cd_tab"], at("cd_tab", l) + 64)
                pe.wait_ge(S["pooled"], at("pooled", l) + 2)
                for j in range(2):
                    for c, (c0, c1) in enumerate(sp0):
                        n = j * len(sp0) + c
                        if n >= 2:
                            pe.wait_ge(S["pool_done"], at("pool_done", l) + n - 1)
                        mm(PS[:, 6 + n % 2, 0:c1 - c0], wpool[:, j, :], R[:, Y + 2 + j, c0:c1],
                           start=True, stop=True).then_inc(S["pool_ps"], 1)
                nconv = TAPS * 2 * len(segs(l))
                pe.wait_ge(S["conv"], at("conv", l) + nconv)
                pe.wait_ge(S["slot_free"], u0 + 16)
                for c0, c1 in sp0:
                    for j in range(2):
                        last = mm(slot(0, t0)[:, c0 - t0:c1 - t0], ones[:, :], R[:, Y + 6 + j, c0:c1],
                                  start=(j == 0), stop=(j == 1))
                last.then_inc(S["mean_ps"], 1)
                pe.wait_ge(S["cd_sq"], at("cd_sq", l) + 2)
                for c0, c1 in sp0:
                    for j in range(2):
                        last = mm(slot(1, t0)[:, c0 - t0:c1 - t0], ones[:, :], xrow(j)[:, c0:c1],
                                  start=(j == 0), stop=(j == 1))
                last.then_inc(S["var_ps"], 1)
                pe.wait_ge(S["silu"], at("silu", l) + 2)
                pe.wait_ge(S["pool_done"], at("pool_done", l) + 2 * len(sp0))
                for e in range(2):
                    for c, (c0, c1) in enumerate(sp0):
                        n = e * len(sp0) + c
                        if n >= 2:
                            pe.wait_ge(S["pw_done"], at("pw_done", l) + n - 1)
                        for k in range(2):
                            last = mm(PS[:, 6 + n % 2, 0:c1 - c0], wpw[:, k, e * P:(e + 1) * P], xrow(k)[:, c0:c1],
                                      start=(k == 0), stop=(k == 1))
                        last.then_inc(S["pw_ps"], 1)
                for i, row in enumerate((G, G + 1, G + 4, G + 5)):
                    tr = 0 if i < 2 else t0
                    if i >= 2:
                        pe.wait_ge(S["roped"], at("roped", l) + i - 1)
                    for c0, c1 in spans(tr):
                        last = mm(slot(i % 2, tr)[:, c0 - tr:c1 - tr], perm[:, :], R[:, row, c0:c1],
                                  start=True, stop=True)
                    last.then_inc(S["roped_ps"], 1)

                def tok_turn(i):
                    t = B_ORDER[i]
                    if i == 0:
                        pe.wait_ge(S["roped"], at("roped", l) + 4)
                        pe.wait_ge(S["pw_done"], at("pw_done", l) + 2 * len(sp0))
                    elif i >= 2:
                        pe.wait_ge(S["k_tok"], at("k_tok", l) + i - 1)
                    for q, row in enumerate((G + 2, G + 3, G, G + 1)):
                        last = nc.tensor.transpose(PS[:, (6, 3)[i % 2], q * P:(q + 1) * P], R[:, row, t * P:(t + 1) * P],
                                                   ident[:, :])
                    last.then_inc(S["tr_ps"], 1)

                def products(i):
                    pe.wait_ge(S["vw"], at("vw", l) + i + 1)
                    pe.wait_ge(S["k_tok"], at("k_tok", l) + i + 1)
                    if i >= 2:
                        pe.wait_ge(S["state"], at("state", l) + i - 1)
                        pe.wait_ge(S["kv_fwd"], at("kv_fwd", l) + fwd_products(i - 2))
                    for dr, vw in enumerate((T[:, 512:1024], vw_fwd)):
                        for q in range(2):
                            if (i < NTILE - 1, B_ORDER[i] < NTILE - 1)[dr]:
                                last = mm(PS[:, KV_BANKS[dr][i % 2], q * P:(q + 1) * P],
                                          T[:, (i % 2) * 256 + q * P:(i % 2) * 256 + (q + 1) * P],
                                          vw[:, (i % 2) * 256 + q * P:(i % 2) * 256 + (q + 1) * P], start=True, stop=True)
                    last.then_inc(S["kv_ps"], 1)

                tok_turn(0)
                for i in range(NTILE):
                    if i + 1 < NTILE:
                        tok_turn(i + 1)
                    products(i)

                tq = t0 // P

                def inner_scores(t):
                    if t == tq:
                        pe.wait_ge(S["state"], at("state", l) + NTILE - 1)
                        pe.wait_ge(S["kv_fwd"], at("kv_fwd", l) + NTILE - 1)
                    else:
                        pe.wait_ge(S["masked"], at("masked", l) + t - tq)
                    for h in range(HB):
                        b, q = 64 * (h % 2), h // 2
                        last = mm(PS[:, 4 * (h % 2), q * P:(q + 1) * P], R[b:b + 64, G + q, t * P:(t + 1) * P],
                                  R[b:b + 64, G + 4 + q, t * P:(t + 1) * P], start=True, stop=True)
                    last.then_inc(S["sc_ps"], 1)

                def retained_out(t):
                    n = t - tq
                    if n:
                        pe.wait_ge(S["y_mid"], at("y_mid", l) + n)
                    if t == 0:
                        pe.wait_ge(S["states_zero"], at("states_zero", l) + 1)
                    else:
                        pe.wait_ge(S["state_fwd"], at("state_fwd", l) + t)
                    for dr in range(2):
                        for h in range(HB):
                            b, q = 64 * (h % 2), h // 2
                            mm(PS[:, 2 + 3 * (h % 2), dr * P + q * 64:dr * P + (q + 1) * 64],
                               R[b:b + 64, G + 4 + q, t * P:(t + 1) * P],
                               (Sf, Sb)[dr][b:b + 64, t, q * 64:(q + 1) * 64], start=True, stop=True)
                    pe.wait_ge(S["masked"], at("masked", l) + n + 1)
                    for dr in range(2):
                        for h in range(HB):
                            last = mm(PS[:, 1, dr * 256 + h * 64:dr * 256 + (h + 1) * 64], pmask[:, dr, h, :],
                                      vtok[:, t, h * 64:(h + 1) * 64], start=True, stop=True)
                    last.then_inc(S["y_ps"], 1)

                def turned_out(n):
                    pe.wait_ge(S["y_norm"], at("y_norm", l) + n + 1)
                    if n:
                        pe.wait_ge(S["yb_sum"], at("yb_sum", l) + n)
                    for q in range(4):
                        last = nc.tensor.transpose(PS[:, 3, q * P:(q + 1) * P], ysum[n % 2][:, q * P:(q + 1) * P], ident[:, :])
                    last.then_inc(S["yt_ps"], 1)

                inner_scores(tq)
                for t in range(tq, NTILE):
                    retained_out(t)
                    if t < NTILE - 1:
                        inner_scores(t + 1)
                    if t > tq:
                        turned_out(t - tq - 1)
                turned_out(NTILE - tq - 1)

                pe.wait_ge(S["a_tab"], at("a_tab", l) + 64)
                pe.wait_ge(S["yb_sum"], at("yb_sum", l) + NTILE - tq)
                for u in range(A_UNITS):
                    gemm_unit(u0 + 16 + u, u % 2, KD, U, 0 if u < 2 or u >= 4 else t0)
                    for m, (i, c0, c1) in enumerate(rotary(l)):
                        if i == u - 1:
                            pe.wait_ge(S["slot_free"], u0 + 16 + u)
                            if m >= 2:
                                pe.wait_ge(S["rot"], at("rot", l) + m - 1)
                            mm(PS[:, 6 + m % 2, 0:c1 - c0], perm[:, :], arow(i)[:, c0:c1],
                               start=True, stop=True).then_inc(S["perm_ps"], 1)
                pe.wait_ge(S["rot"], at("rot", l) + len(rotary(l)))
                for n, (m, i, j, c0, c1) in enumerate(stacks(l)):
                    w = c1 - c0
                    pe.wait_ge(S["rot_lo"], at("rot_lo", l) + m + 1)
                    if n == 2:
                        pe.wait_ge(S["slot_free"], u0 + NIN)
                    if n >= 4:
                        pe.wait_ge(S["stk_dve" if n % 2 else "stk_act"], at("stk_act", l) + n // 2 - 1)
                    for x in range(2):
                        col = 192 + 32 * x if i < 2 else 64 * x
                        last = mm(PS[:, STACK_BANKS[n % 4], 0:w], stk[:, j, col:col + P],
                                  arow16(i, 2 * c0 + x * w, 2 * c0 + (x + 1) * w), start=(x == 0), stop=(x == 1))
                    last.then_inc(S["stk_ps"], 1)
                for t in range(NTILE):
                    if t >= 4:
                        pe.wait_ge(S["vt_done"], at("vt_done", l) + t - 3)
                    for q in range(2):
                        last = nc.tensor.transpose(PS[:, VALUE_BANKS[t % 4], q * P:(q + 1) * P],
                                                   arow(4 + q)[:, t * P:(t + 1) * P], ident[:, :])
                    last.then_inc(S["vt_ps"], 1)
                for n in ("stk_act", "stk_dve"):
                    pe.wait_ge(S[n], at(n, l) + len(stacks(l)) // 2)
                pe.wait_ge(S["vt_done"], at("vt_done", l) + NTILE)
                for run, t_first, nt, nk in attend_runs(l):
                    attend(l, run, t_first, nt, nk)
                    pe.wait_ge(S[f"ot_done_{run}{l}"], nt)

                gemm(unit0(l, "out"), KD, KD, Y, t0)
                pe.wait_ge(S["slot_free"], unit0(l, "out") + KD)
                sum_rows(4 * l + 1, t0)
                pe.wait_ge(S["root"], 4 * l + 2)
                sum_rows(4 * l + 2, t0)
                pe.wait_ge(S["u_done"], 2 * KD * (l + 1))
                for q, nf in enumerate(FPARTS):
                    with_ada = l == 0 and q == 0
                    gemm(unit0(l, "gu", q), 2 * nf, KD, U, t0,
                         *([ffn_modulation] if with_ada else []))
                    pe.wait_ge(S["ffn_lo"], at("ffn_lo", l) + sum(FPARTS[:q + 1]))
                    gemm(unit0(l, "down", q), KD, nf, G, t0,
                         *([lambda i, j, r: ffn_modulation(i + 2 * nf, j, r + nf)] if with_ada else []))
                pe.wait_ge(S["slot_free"], unit0(l + 1, "in"))
                sum_rows(4 * l + 3, t0)
                if l < LAYERS - 1:
                    pe.wait_ge(S["root"], 4 * l + 4)
                    sum_rows(4 * l + 4, t0)

        @block.scalar
        def _(act):
            A = nc.scalar.activation
            own = Chain(act, S["act_own"])

            def hi_part(v, j, K):
                act.wait_ge(w_landed[j], 8 * v + (16 - 8 * j))
                if not (isinstance(v, int) and v < 2):
                    act.wait_ge(S["units"], v - 1)
                A(whi[:, j, 0:K, :], stage[:, j, 0:K, :], ACT.Copy, scale=WS).then_inc(S["w_hi"], 1)

            def units(u0, n, evac):
                def body(i, j, r):
                    nxt = u0 + i + 1
                    if isinstance(i, int):
                        if nxt < len(UK):
                            hi_part(nxt, 1 - j, UK[nxt])
                    else:
                        hi_part(nxt, 1 - j, UK[u0 + 1])
                    act.wait_ge(S["units"], nxt)
                    evac(i, j, r)
                pairs(act, n, body)

            def root(inst, t0):
                act.wait_ge(S["sumsq"], inst + 1)
                A(xrow(1)[:, t0:], slot(0, t0), ACT.Sqrt, scale=1.0 / D, bias=epsv[:, 0:1]).then_inc(S["root"], 1)

            def squares_of_h(inst, t0, first_rows):
                for d in range(KD):
                    q = KD * inst + d
                    act.wait_ge(S["h_rows"], first_rows + d + 1)
                    act.wait_ge(S["sq_used"], q - 1)
                    A(xrow(2 + d % 2)[:, t0:], R[:, H + d, t0:], ACT.Square).then_inc(S["sq_ready"], 1)

            def modulate(l, norm, t0):
                for d in range(KD):
                    act.wait_ge(S["u_scaled"], KD * (2 * l + norm) + d + 1)
                    row = xrow(2 + d % 2)
                    for st, c0, c1 in streams(t0):
                        last = A(row[:, c0:c1], row[:, c0:c1], ACT.Identity,
                                 scale=vv(l, 0, norm, st, d), bias=vv(l, 1, norm, st, d))
                    own.link(last)
                    A(hl(U + d, 0, t0, TOK), row[:, t0:], ACT.Copy).then_inc(S["u_hi"], 1)

            def attend(l, run, t_first, nt, nk):
                s = lambda n: S[f"{n}_{run}{l}"]
                groups = key_groups(nk)
                NG, keys = len(groups), nk * P

                def exps(r, h, c):
                    n = 4 * r + h
                    act.wait_ge(s("nbias"), 2 * n + (c + 1))
                    if not (isinstance(r, int) and n < 2):
                        act.wait_ge(s("w"), n - 1)
                    A((P1, P2)[c][h % 2][:, 0:keys], slot(c)[:, 0:keys], ACT.Exp, scale=SCORE,
                      bias=nbias[:, h % 2, c:c + 1], accum_out=den[:, h % 2, c:c + 1]).then_inc(s("exps"), 1)

                def wt_hi(r, h, p):
                    n = 4 * r + h
                    w = groups[p][1] * P
                    act.wait_ge(s("wt_ps"), NG * n + (p + 1))
                    if p or not (isinstance(r, int) and n < 2):
                        if not (isinstance(r, int) and n == 0):
                            act.wait_ge(s("pv"), NG * n + (p + 1 - (NG if p else 2 * NG)))
                    A(WTb(h, p)[:, 0, 0:w], turned(p, w), ACT.Copy).then_inc(s("wt_hi"), 1)

                def out_hi(r):
                    act.wait_ge(s("ot_ps"), r + 1)
                    A(hlr(Y, 2, 0, (t_first + r) * P, P), PS[:, 6, 0:256].rearrange("p (j t) -> p j t", j=2),
                      ACT.Copy, scale=sm(l, "g_sub")).then_inc(s("ot_hi"), 1)

                def tile(r, first=False):
                    for h in range(HA):
                        if h >= 2 or not first:
                            for p in range(1, NG):
                                wt_hi(*back(r, h, 2), p)
                        exps(r, h, 0)
                        if h == 2 and not first:
                            out_hi(r - 1)
                        if h or not first:
                            wt_hi(*back(r, h, 1), 0)
                        exps(r, h, 1)

                tile(0, first=True)
                with act.Fori(1, nt) as r:
                    tile(r)
                for p in range(1, NG):
                    wt_hi(nt - 1, HA - 2, p)
                for p in range(NG):
                    wt_hi(nt - 1, HA - 1, p)
                out_hi(nt - 1)

            act.wait_ge(S["smalls"], 64)
            A(T[:, 768:784], csil[:, :, :].rearrange("p k s -> p (k s)"), ACT.Tanh, scale=0.5).then_inc(S["c_tanh"], 1)
            act.wait_ge(S["lam_dots"], 1)
            A(lamv[:, 4:8], lamv[:, 0:4], ACT.Exp).then_inc(S["lam_exp"], 1)
            act.wait_ge(S["h_in"], 16 * KD)
            for d in range(KD):
                if d >= 2:
                    act.wait_ge(S["sq_used"], d - 1)
                A(xrow(2 + d % 2), R[:, H + d, :], ACT.Square).then_inc(S["sq_ready"], 1)
            act.wait_ge(S["small_const"], 3)
            root(0, 0)
            hi_part(0, 0, UK[0])

            for l in range(LAYERS):
                t0 = first_tok(l)
                sp0 = spans(t0)
                u0 = unit0(l, "in")
                act.wait_ge(S["vec_ready"], 2 * l + 1)
                modulate(l, 0, t0 * 0)

                def cd_evac(i, j, r):
                    kind, dst = ((ACT.Copy, Gpad[:, 2 + j, :]), (ACT.Tanh, Gpad[:, j, :]), (ACT.Copy, Xpad[:, j, :]))[r]
                    for p0, c0, n in segs(l):
                        last = A(dst[:, p0:p0 + n], slot(j, t0)[:, c0 - t0:c0 - t0 + n], kind,
                                 scale=UNS if r == 0 else UNS * 0.5)
                    last.then_inc(S["slot_free"], 1)

                for r in range(CD_UNITS // 2):
                    for j in range(2):
                        u = u0 + 2 * r + j
                        hi_part(u + 1, 1 - j, KD)
                        act.wait_ge(S["units"], u + 1)
                        cd_evac(2 * r + j, j, r)

                act.wait_ge(S["glu"], at("glu", l) + 2)
                act.wait_ge(S["pooled"], at("pooled", l) + 2)
                units(u0 + 6, 4, lambda i, j, r: A(R[:, bass.ds(G + i, 1), :], slot(j), ACT.Copy,
                                                   scale=UNS).then_inc(S["slot_free"], 1))
                units(u0 + 10, 2, lambda i, j, r: A(R[:, G + 4 + i, t0:], slot(j, t0), ACT.Copy,
                                                    scale=UNS).then_inc(S["slot_free"], 1))
                units(u0 + 12, 4, lambda i, j, r: A(R[:, bass.ds(G + 6 + i, 1), t0:], slot(j, t0), ACT.Tanh,
                                                    scale=UNS * 0.5).then_inc(S["gate_tanh"], 1))

                for j in range(2):
                    for c, (c0, c1) in enumerate(sp0):
                        n = j * len(sp0) + c
                        act.wait_ge(S["pool_ps"], at("pool_ps", l) + n + 1)
                        A(hl(Y + 4 + j, 0, c0, c1), PS[:, 6 + n % 2, 0:c1 - c0], ACT.Copy,
                          scale=sm(l, "s_pool", j)).then_inc(S["pool_hi"], 1)
                for j in range(2):
                    act.wait_ge(S["centered"], at("centered", l) + j + 1)
                    A(xrow(j)[:, t0:], R[:, Y + 6 + j, t0:], ACT.Square).then_inc(S["cd_sq"], 1)
                act.wait_ge(S["var_ps"], at("var_ps", l) + 1)
                A(xrow(2)[:, t0:], slot(1, t0), ACT.Sqrt, scale=1.0 / 256, bias=epsv[:, 1:2]).then_inc(S["ln_root"], 1)
                for j in range(2):
                    act.wait_ge(S["zed"], at("zed", l) + j + 1)
                    A(xrow(j)[:, t0:], R[:, Y + 6 + j, t0:], ACT.Tanh, scale=0.5).then_inc(S["zed_tanh"], 1)
                for e in range(2):
                    for c, (c0, c1) in enumerate(sp0):
                        n = e * len(sp0) + c
                        act.wait_ge(S["pw_ps"], at("pw_ps", l) + n + 1)
                        A(hl(Y + 6 + e, 0, c0, c1), PS[:, 6 + n % 2, 0:c1 - c0], ACT.Copy,
                          scale=XS * 0.5).then_inc(S["pw_hi"], 1)

                def forward_product(i):
                    t = B_ORDER[i]
                    act.wait_ge(S["kv_ps"], at("kv_ps", l) + i + 1)
                    if t < NTILE - 1:
                        for b in (0, 64):
                            last = A(Sf[b:b + 64, t + 1, :].rearrange("p (q e) -> p q e", q=2),
                                     PS[b:b + 64, KV_BANKS[1][i % 2], 0:256].rearrange("p (q e) -> p q e", q=2)[:, :, b:b + 64],
                                     ACT.Copy)
                        last.then_inc(S["kv_fwd"], 1)

                for i in range(NTILE):
                    act.wait_ge(S["tr_ps"], at("tr_ps", l) + i + 1)
                    A(vtok[:, B_ORDER[i], :], PS[:, (6, 3)[i % 2], 0:256], ACT.Copy).then_inc(S["v_tok"], 1)
                    if i >= 2:
                        act.wait_ge(S["kv_ps"], at("kv_ps", l) + i - 1)
                    A(T[:, (i % 2) * 256:(i % 2) * 256 + 256], PS[:, (6, 3)[i % 2], 256:512], ACT.Copy).then_inc(S["k_tok"], 1)
                    if i:
                        forward_product(i - 1)
                forward_product(NTILE - 1)
                tq = t0 // P
                act.wait_ge(S["kv_ps"], at("kv_ps", l) + NTILE)

                def gated_hi(n):
                    t = n + tq
                    act.wait_ge(S["yb_sum"], at("yb_sum", l) + n + 1)
                    A(hlr(Y + 2, 2, 0, t * P, P), R[:, G + 6:G + 8, t * P:(t + 1) * P], ACT.Copy,
                      scale=XS * 0.5 * UNS).then_inc(S["yb_hi"], 1)

                for n in range(NTILE - tq):
                    if n >= 2:
                        gated_hi(n - 2)
                    act.wait_ge(S["y_mid"], at("y_mid", l) + n + 1)
                    if n:
                        act.wait_ge(S["y_var"], at("y_var", l) + n)
                    A(SW[:, 0:512], ysum[n % 2], ACT.Square).then_inc(S["y_sq"], 1)
                for n in (NTILE - tq - 2, NTILE - tq - 1):
                    gated_hi(n)

                for v in range(A_UNITS):
                    u = u0 + 16 + v
                    hi_part(u + 1, 1 - v % 2, KD)
                    act.wait_ge(S["units"], u + 1)
                    if v < 4:
                        tr = 0 if v < 2 else t0
                        A(arow(v)[:, tr:TOK], slot(v % 2, tr), ACT.Copy, scale=UNS * XS).then_inc(S["slot_free"], 1)
                    elif v == 5:
                        for j in range(2):
                            A(arow(4 + j), slot(j), ACT.Copy, scale=UNS * XS).then_inc(S["slot_free"], 1)
                    for m, (i, c0, c1) in enumerate(rotary(l)):
                        if i == v - 1:
                            act.wait_ge(S["rot"], at("rot", l) + m + 1)
                            A(arow16(i, 2 * c0, c0 + c1), T[:, 512:512 + c1 - c0], ACT.Copy).then_inc(S["rot_hi"], 1)
                for n, (m, i, j, c0, c1) in enumerate(stacks(l)):
                    if n % 2 == 0:
                        act.wait_ge(S["stk_ps"], at("stk_ps", l) + n + 1)
                        A((Kst, Qst)[i // 2][:, 4 * (i % 2) + j, c0:c1], PS[:, STACK_BANKS[n % 4], 0:c1 - c0],
                          ACT.Copy).then_inc(S["stk_act"], 1)
                for t in range(NTILE):
                    act.wait_ge(S["vt_ps"], at("vt_ps", l) + t + 1)
                    A(Vst[:, t, :, 0, :], PS[:, VALUE_BANKS[t % 4], 0:256].rearrange("p (h e) -> p h e", h=HA),
                      ACT.Copy).then_inc(S["vt_hi"], 1)
                for run, t_first, nt, nk in attend_runs(l):
                    attend(l, run, t_first, nt, nk)

                def out_evac(i, j, r):
                    act.wait_ge(S["sq_used"], i + (KD * (4 * l + 1) - 1))
                    A(xrow(2 + j)[:, t0:], slot(j, t0), ACT.Square, scale=UNS).then_inc(S["sq_ready"], 1)
                    A(R[:, bass.ds(U + i, 1), t0:], slot(j, t0), ACT.Copy, scale=UNS).then_inc(S["slot_free"], 1)

                units(unit0(l, "out"), KD, out_evac)
                root(4 * l + 1, t0)
                squares_of_h(4 * l + 2, t0, 2 * KD * l)
                root(4 * l + 2, t0)
                act.wait_ge(S["vec_ready"], 2 * l + 2)
                modulate(l, 1, t0)

                done = 0
                for q, nf in enumerate(FPARTS):
                    def ffn_evac(i, j, r):
                        if j == 0:
                            act.wait_ge(S["slot_free"], i + (unit0(l, "gu", q) - 1))
                            A(xrow(1)[:, t0:], slot(0, t0), ACT.Tanh, scale=UNS * 0.5).then_inc(S["g_tanh"], 1)
                        else:
                            act.wait_ge(S["slot_free"], i + (unit0(l, "gu", q) + 1))
                            A(hlr(G + r, 1, 0, t0, TOK - t0) if isinstance(r, int) else
                              R16[:, bass.ds(G + r, 1), t0:TOK], xrow(3)[:, t0:], ACT.Copy).then_inc(S["ffn_hi"], 1)

                    def down_evac(i, j, r):
                        if q == 0:
                            A(R[:, bass.ds(Y + i, 1), t0:], slot(j, t0), ACT.Copy, scale=UNS).then_inc(S["slot_free"], 1)
                        elif q == len(FPARTS) - 1:
                            act.wait_ge(S["slot_free"], i + (unit0(l, "down", q) + 1))
                            act.wait_ge(S["sq_used"], i + (KD * (4 * l + 3) - 1))
                            A(xrow(2 + j)[:, t0:], R[:, bass.ds(Y + i, 1), t0:], ACT.Square).then_inc(S["sq_ready"], 1)

                    units(unit0(l, "gu", q), 2 * nf, ffn_evac)
                    units(unit0(l, "down", q), KD, down_evac)
                    done += nf
                root(4 * l + 3, t0)
                if l < LAYERS - 1:
                    squares_of_h(4 * l + 4, t0, 2 * KD * l + KD)
                    root(4 * l + 4, t0)

        @block.vector
        def _(dve):
            TS, TT, STT = nc.vector.tensor_scalar, nc.vector.tensor_tensor, nc.vector.scalar_tensor_tensor
            RED = nc.vector.tensor_reduce
            own = Chain(dve, S["dve_own"])

            def lo_part(v, j, K):
                dve.wait_ge(S["w_hi"], v + 1)
                STT(wlo[:, j, 0:K, :], stage[:, j, 0:K, :], WS, whi[:, j, 0:K, :],
                    ALU.mult, ALU.subtract).then_inc(S["w_lo"], 1)

            def units(u0, n, evac, wait=True):
                def body(i, j, r):
                    nxt = u0 + i + 1
                    if isinstance(i, int):
                        if nxt < len(UK):
                            lo_part(nxt, 1 - j, UK[nxt])
                    else:
                        lo_part(nxt, 1 - j, UK[u0 + 1])
                    evac(i, j, r)
                pairs(dve, n, body)

            def inverse_root(inst, t0):
                dve.wait_ge(S["root"], inst + 1)
                own.link(nc.vector.reciprocal(xrow(1)[:, t0:], xrow(1)[:, t0:]))

            def scale_rows(l, norm, t0):
                base = KD * (2 * l + norm)
                def lo(d):
                    dve.wait_ge(S["u_hi"], base + d + 1)
                    TT(hl(U + d, 1, t0, TOK), xrow(2 + d % 2)[:, t0:], hl(U + d, 0, t0, TOK),
                       ALU.subtract).then_inc(S["u_done"], 1)
                for d in range(KD):
                    if d >= 2:
                        dve.wait_ge(S["u_done"], base + d - 1)
                    else:
                        dve.wait_ge(S["sq_used"], KD * (4 * l + 2 * norm + 1))
                    TT(xrow(2 + d % 2)[:, t0:], R[:, H + d, t0:], xrow(1)[:, t0:], ALU.mult).then_inc(S["u_scaled"], 1)
                    if d:
                        lo(d - 1)
                lo(KD - 1)

            def add_to_h(l, norm, row0, t0):
                TT(R[:, row0, t0:], R[:, row0, t0:], xrow(1)[:, t0:], ALU.mult).then_inc(S["dve_own"], 1)
                own.k += 1
                for d in range(KD):
                    mark = own.base + own.k
                    if d + 1 < KD:
                        TT(R[:, row0 + d + 1, t0:], R[:, row0 + d + 1, t0:], xrow(1)[:, t0:],
                           ALU.mult).then_inc(S["dve_own"], 1)
                        own.k += 1
                    dve.wait_ge(S["dve_own"], mark)
                    for st, c0, c1 in streams(t0):
                        last = STT(R[:, H + d, c0:c1], R[:, row0 + d, c0:c1], vv(l, 2, norm, st, d),
                                   R[:, H + d, c0:c1], ALU.mult, ALU.add)
                    last.then_inc(S["h_rows"], 1)

            def attend(l, run, t_first, nt, nk):
                s = lambda n: S[f"{n}_{run}{l}"]
                groups = key_groups(nk)
                NG, keys = len(groups), nk * P

                def maxima(r, h, c):
                    n = 4 * r + h
                    dve.wait_ge(s("scores"), 2 * n + (c + 1))
                    own.link(RED(smax[:, h % 2, c:c + 1], slot(c)[:, 0:keys], AX.X, ALU.max))
                    if not (isinstance(r, int) and n < 2):
                        dve.wait_ge(s("exps"), 2 * n + (c - 3))
                    TS(nbias[:, h % 2, c:c + 1], smax[:, h % 2, c:c + 1], -SCORE, lamv[:, 12 + l:13 + l] if c == 0 else None,
                       ALU.mult, ALU.add if c == 0 else ALU.bypass).then_inc(s("nbias"), 1)

                def wt_lo(r, h, p):
                    n = 4 * r + h
                    w = groups[p][1] * P
                    dve.wait_ge(s("wt_hi"), NG * n + (p + 1))
                    TT(WTb(h, p)[:, 1, 0:w], turned(p, w), WTb(h, p)[:, 0, 0:w], ALU.subtract).then_inc(s("wt_lo"), 1)

                def combine(r, h):
                    n = 4 * r + h
                    dve.wait_ge(s("exps"), 2 * n + 2)
                    d1, d2 = den[:, h % 2, 0:1], den[:, h % 2, 1:2]
                    TS(rl[:, h:h + 1], d1, XS, None, ALU.mult)
                    own.link(nc.vector.reciprocal(beta[:, 1:2], d2))
                    own.link(STT(beta[:, 0:1], d1, lamv[:, 10 + l:11 + l], beta[:, 1:2], ALU.mult, ALU.mult))
                    if not (isinstance(r, int) and n < 2):
                        dve.wait_ge(s("wt_ps"), NG * n - NG)
                    STT(Wt[h % 2][:, 0:keys], P2[h % 2][:, 0:keys], beta[:, 0:1], P1[h % 2][:, 0:keys],
                        ALU.mult, ALU.add).then_inc(s("w"), 1)
                    if h == HA - 1:
                        own.link(nc.vector.reciprocal(rinv[:, :], rl[:, :]))

                def out_sum(r):
                    dve.wait_ge(s("pv"), NG * (4 * r + 4))
                    TT(AO[:, 0, :, :], PS[:, 7, 0:256].rearrange("p (h e) -> p h e", h=HA),
                       rinv[:, :].rearrange("p (h e) -> p h e", e=1).to_broadcast([P, HA, DV]), ALU.mult).then_inc(s("o_sum"), 1)
                    dve.wait_ge(s("o_sum"), r + 1)
                    own.link(TT(AO[:, 1, :, :], AO[:, 0, :, :], AO[:, 0, :, :], ALU.mult))
                    own.link(RED(st8[:, 0, 0:4], AO[:, 1, :, :], AX.X, ALU.add))
                    TS(st8[:, 1, 0:4], st8[:, 0, 0:4], 1.0 / DV, 1e-5, ALU.mult, ALU.add).then_inc(s("o_var"), 1)

                def out_norm(r):
                    dve.wait_ge(s("o_pow"), r + 1)
                    if not (isinstance(r, int) and r == 0):
                        dve.wait_ge(s("ot_ps"), r)
                    TT(AO[:, 2, :, :], AO[:, 0, :, :], st8[:, 2, 0:4].rearrange("p (h e) -> p h e", e=1).to_broadcast([P, HA, DV]),
                       ALU.mult).then_inc(s("o_norm"), 1)

                def out_lo(r):
                    dve.wait_ge(s("ot_hi"), r + 1)
                    STT(hlr(Y, 2, 1, (t_first + r) * P, P), PS[:, 6, 0:256].rearrange("p (j t) -> p j t", j=2),
                        sm(l, "g_sub"), hlr(Y, 2, 0, (t_first + r) * P, P), ALU.mult, ALU.subtract).then_inc(s("ot_done"), 1)

                def tile(r, first=False):
                    for h in range(HA):
                        maxima(r, h, 0)
                        if h >= 2 or not first:
                            for p in range(1, NG):
                                wt_lo(*back(r, h, 2), p)
                        if h == 2 and not first:
                            out_norm(r - 1)
                        if h or not first:
                            combine(*back(r, h, 1))
                        if h == 2 and not first:
                            out_lo(r - 1)
                        maxima(r, h, 1)
                        if h or not first:
                            wt_lo(*back(r, h, 1), 0)
                        if h == 1 and not first:
                            out_sum(r - 1)

                per = 8 + 8 + 1 + 2
                tile(0, first=True)
                with dve.Fori(1, nt) as r:
                    own.enter(r - 1, per)
                    tile(r)
                own.leave(nt - 1, per)
                for p in range(1, NG):
                    wt_lo(nt - 1, HA - 2, p)
                combine(nt - 1, HA - 1)
                for p in range(NG):
                    wt_lo(nt - 1, HA - 1, p)
                out_sum(nt - 1)
                out_norm(nt - 1)
                out_lo(nt - 1)

            def modulation(group, first, n, col):
                dve.wait_ge(S["ada_used"], first + n)
                dve.wait_ge(S["b_ada"], 16 * group + 16)
                mod = T[:, 384:384 + 2 * n]
                own.link(TT(mod.rearrange("p (m s) -> p m s", s=2), PSF[:, col:col + 2 * n].rearrange("p (m s) -> p m s", s=2),
                            bada[:, 0:n].rearrange("p (m s) -> p m s", s=1).to_broadcast([P, n, 2]), ALU.add))
                for b in range(n // KD):
                    l, m = divmod(first // KD + b, 6)
                    norm, kind = divmod(m, 3)
                    src = mod[:, 2 * KD * b:2 * KD * (b + 1)].rearrange("p (d s) -> p s d", s=2)
                    gain = sm(l, "g_post" if kind == 2 else "g_pre", KD * norm, KD).rearrange(
                        "p (s d) -> p s d", s=1).to_broadcast([P, 2, KD])
                    if kind == 0:
                        last = TS(vec[:, l, 1, norm], src, XS, None, ALU.mult)
                    elif kind == 1:
                        own.link(STT(vec[:, l, 0, norm], src, 1.0, gain, ALU.add, ALU.mult))
                        last = TS(vec[:, l, 0, norm], vec[:, l, 0, norm], XS, None, ALU.mult)
                    else:
                        last = TT(vec[:, l, 2, norm], src, gain, ALU.mult)
                last.then_inc(S["vec_ready"], 1)

            dve.wait_ge(S["smalls"], 64)
            lamq = T[:, 0:256].rearrange("p (m x e) -> p m x e", m=4, x=2)
            own.link(TT(T[:, 256:384].rearrange("p (m e) -> p m e", m=4), lamq[:, :, 0, :], lamq[:, :, 1, :], ALU.mult))
            RED(lamv[:, 0:4], T[:, 256:384].rearrange("p (m e) -> p m e", m=4), AX.X, ALU.add).then_inc(S["lam_dots"], 1)
            dve.wait_ge(S["c_tanh"], 1)
            cs = csil[:, :, :].rearrange("p k s -> p (k s)")
            own.link(STT(cs, T[:, 768:784], 1.0, cs, ALU.add, ALU.mult))
            TS(cs, cs, 0.5, None, ALU.mult).then_inc(S["csil"], 1)
            dve.wait_ge(S["lam_exp"], 1)
            dve.wait_ge(S["lam_dots"], 1)
            e2 = lamv[:, 4:8].rearrange("p (l x) -> p l x", x=2)
            s2 = lamv[:, 0:4].rearrange("p (l x) -> p l x", x=2)
            own.link(TT(lamv[:, 8:10], e2[:, :, 0], e2[:, :, 1], ALU.subtract))
            own.link(TT(lamv[:, 14:16], s2[:, :, 0], s2[:, :, 1], ALU.max))
            for l in range(LAYERS):
                own.link(TS(lamv[:, 10 + l:11 + l], lamv[:, 8 + l:9 + l], -1.0, -LAM_INIT[l], ALU.mult, ALU.add))
                own.link(TS(sm(l, "g_sub"), sm(l, "g_sub"), XS * (1.0 - LAM_INIT[l]), None, ALU.mult))
                own.link(TS(sm(l, "s_pool", 0, 2), sm(l, "s_pool", 0, 2), XS, None, ALU.mult))
            own.link(TS(lamv[:, 12:14], lamv[:, 14:16], 0.0, -1.0, ALU.max, ALU.mult))
            lo_part(0, 0, UK[0])
            inverse_root(0, 0)
            modulation(0, 0, ADA_FIRST, 3072)

            for l in range(LAYERS):
                t0 = first_tok(l)
                sp0 = spans(t0)
                u0 = unit0(l, "in")
                scale_rows(l, 0, 0)
                for i in range(CD_UNITS):
                    lo_part(u0 + i + 1, (i + 1) % 2, KD)
                dve.wait_ge(S["slot_free"], u0 + 6)
                for j in range(2):
                    for p0, c0, n in segs(l):
                        last = STT(Xpad[:, j, p0:p0 + n], Gpad[:, j, p0:p0 + n], 1.0, Xpad[:, j, p0:p0 + n],
                                   ALU.add, ALU.mult)
                    last.then_inc(S["glu"], 1)
                dve.wait_ge(S["glu"], at("glu", l) + 2)
                dve.wait_ge(S["pads_zero"], at("pads_zero", l) + 1)
                lanes = [(j, sg) for j in range(2) for sg in segs(l)]
                NL = len(lanes)

                def tap(n):
                    for x, (j, (p0, c0, w)) in enumerate(lanes):
                        acc = R[:, Y + 6 + j, c0:c0 + w]
                        wv = small[:, l, bass.ds(SM_AT["conv_w"][0] + j * TAPS + n, 1)]
                        src = Xpad[:, j, bass.ds(p0 - HALF + n, w)]
                        if isinstance(n, int) and n == 0:
                            TS(acc, src, wv, sm(l, "conv_b", j), ALU.mult, ALU.add).then_inc(S["conv"], 1)
                        else:
                            dve.wait_ge(S["conv"], at("conv", l) + NL * n + (x + 1 - NL))
                            STT(acc, src, wv, acc, ALU.mult, ALU.add).then_inc(S["conv"], 1)

                tap(0)

                def b_step(first_tap, gate, row0):
                    def f(i, j, r):
                        for x in range(3):
                            tap(3 * i + (first_tap + x))
                        if gate:
                            dve.wait_ge(S["gate_tanh"], at("gate_tanh", l) + i + 1)
                            row = R[:, bass.ds(G + 6 + i, 1), t0:]
                            STT(row, row, 1.0, slot(j, t0).rearrange("p (a t) -> p a t", a=1),
                                ALU.add, ALU.mult).then_inc(S["slot_free"], 1)
                    return f

                units(u0 + 6, 4, b_step(1, False, 0))
                units(u0 + 10, 2, b_step(13, False, 0))
                units(u0 + 12, 4, b_step(19, True, 0))
                for j in range(2):
                    for c, (c0, c1) in enumerate(sp0):
                        n = j * len(sp0) + c
                        dve.wait_ge(S["pool_hi"], at("pool_hi", l) + n + 1)
                        STT(hl(Y + 4 + j, 1, c0, c1), PS[:, 6 + n % 2, 0:c1 - c0], sm(l, "s_pool", j),
                            hl(Y + 4 + j, 0, c0, c1), ALU.mult, ALU.subtract).then_inc(S["pool_done"], 1)
                dve.wait_ge(S["mean_ps"], at("mean_ps", l) + 1)
                for j in range(2):
                    acc = R[:, Y + 6 + j, t0:]
                    STT(acc, slot(0, t0), -1.0 / 256, acc, ALU.mult, ALU.add).then_inc(S["centered"], 1)
                dve.wait_ge(S["ln_root"], at("ln_root", l) + 1)
                dve.wait_ge(S["centered"], at("centered", l) + 2)
                own.link(nc.vector.reciprocal(xrow(2)[:, t0:], xrow(2)[:, t0:]))
                for j in range(2):
                    acc = R[:, Y + 6 + j, t0:]
                    own.link(TT(acc, acc, xrow(2)[:, t0:], ALU.mult))
                    TS(acc, acc, sm(l, "ln_g", j), sm(l, "ln_b", j), ALU.mult, ALU.add).then_inc(S["zed"], 1)
                for j in range(2):
                    dve.wait_ge(S["zed_tanh"], at("zed_tanh", l) + j + 1)
                    STT(xrow(j)[:, t0:], xrow(j)[:, t0:], 1.0, R[:, Y + 6 + j, t0:],
                        ALU.add, ALU.mult).then_inc(S["silu"], 1)
                for e in range(2):
                    for c, (c0, c1) in enumerate(sp0):
                        n = e * len(sp0) + c
                        dve.wait_ge(S["pw_hi"], at("pw_hi", l) + n + 1)
                        STT(hl(Y + 6 + e, 1, c0, c1), PS[:, 6 + n % 2, 0:c1 - c0], XS * 0.5,
                            hl(Y + 6 + e, 0, c0, c1), ALU.mult, ALU.subtract).then_inc(S["pw_done"], 1)

                dve.wait_ge(S["b_tab"], at("b_tab", l) + 32)
                for i, row in enumerate((G, G + 1, G + 4, G + 5)):
                    tr = 0 if i < 2 else t0
                    dve.wait_ge(S["roped_ps"], at("roped_ps", l) + i + 1)
                    ch = [(c, min(c + 640, TOK)) for c in range(tr, TOK, 640)]
                    for x, (c0, c1) in enumerate(ch):
                        TT(T[:, 0:c1 - c0], slot(i % 2, tr)[:, c0 - tr:c1 - tr], xrow(3)[:, c0:c1], ALU.mult)
                        own.link(TT(R[:, row, c0:c1], R[:, row, c0:c1], xrow(2)[:, c0:c1], ALU.mult))
                        last = TT(R[:, row, c0:c1], R[:, row, c0:c1], T[:, 0:c1 - c0], ALU.add)
                        if x == len(ch) - 1:
                            last.then_inc(S["roped"], 1)
                        else:
                            own.link(last)
                    dve.wait_ge(S["roped"], at("roped", l) + i + 1)

                def by_head(col0, half):
                    return rtab[:, col0 + 4 * half:col0 + 4 * half + 4].rearrange("p (h e) -> p h e", e=1).to_broadcast([P, HB, 64])

                heads = lambda ap: ap.rearrange("p (h e) -> p h e", h=HB)

                def weighted(i):
                    t = B_ORDER[i]
                    dve.wait_ge(S["v_tok"], at("v_tok", l) + i + 1)
                    if i >= 2:
                        dve.wait_ge(S["kv_ps"], at("kv_ps", l) + i - 1)
                    c = (i % 2) * 256
                    TT(heads(T[:, 512 + c:768 + c]), heads(vtok[:, t, :]), by_head(8, 1), ALU.mult)
                    TT(heads(vw_fwd[:, c:c + 256]), heads(vtok[:, t, :]), by_head(8, 0), ALU.mult).then_inc(S["vw"], 1)

                weighted(0)
                for i in range(NTILE - 1):
                    weighted(i + 1)
                    t, nx = B_ORDER[i], B_ORDER[i + 1]
                    dve.wait_ge(S["kv_ps"], at("kv_ps", l) + i + 1)
                    if i:
                        dve.wait_ge(S["state"], at("state", l) + i)
                    else:
                        dve.wait_ge(S["states_zero"], at("states_zero", l) + 1)
                    for q in range(2):
                        for b in (0, 64):
                            last = STT(Sb[b:b + 64, nx, q * 64:(q + 1) * 64], Sb[b:b + 64, t, q * 64:(q + 1) * 64],
                                       g128[b:b + 64, q:q + 1], PS[b:b + 64, KV_BANKS[0][i % 2], q * P + b:q * P + b + 64],
                                       ALU.mult, ALU.add)
                    last.then_inc(S["state"], 1)
                tq = t0 // P
                NQ = NTILE - tq
                y8 = lambda n: ysum[n % 2].rearrange("p (g e) -> p g e", g=8)
                s8 = SW[:, 0:512].rearrange("p (g e) -> p g e", g=8)
                c8 = ycross.rearrange("p (g e) -> p g e", g=8)
                b8 = lambda ap: ap.rearrange("p (g e) -> p g e", e=1).to_broadcast([P, 8, 64])

                def forward_state(t):
                    if t > 1:
                        dve.wait_ge(S["state_fwd"], at("state_fwd", l) + t - 1)
                    for q in range(2):
                        last = STT(Sf[:, t, q * 64:(q + 1) * 64], Sf[:, t - 1, q * 64:(q + 1) * 64], g128[:, q:q + 1],
                                   Sf[:, t, q * 64:(q + 1) * 64], ALU.mult, ALU.add)
                    last.then_inc(S["state_fwd"], 1)

                def masks(n):
                    dve.wait_ge(S["sc_ps"], at("sc_ps", l) + n + 1)
                    if n:
                        dve.wait_ge(S["y_ps"], at("y_ps", l) + n)
                    for x in range(2):
                        last = TT(pmask[:, :, x:HB:2, :],
                                  PS[:, 4 * x, 0:256].rearrange("p (d h c) -> p d h c", d=1, h=2).to_broadcast([P, 2, 2, P]),
                                  dmask[:, :, x:HB:2, :], ALU.mult)
                    last.then_inc(S["masked"], 1)

                def centre(n):
                    dve.wait_ge(S["y_ps"], at("y_ps", l) + n + 1)
                    for x in range(2):
                        last = TT(c8[:, x:8:2, :], PS[:, 2 + 3 * x, 0:256].rearrange("p (g e) -> p g e", g=4),
                                  cross[:, x:8:2].rearrange("p (g e) -> p g e", e=1).to_broadcast([P, 4, 64]), ALU.mult)
                    own.link(last)
                    if n >= 2:
                        dve.wait_ge(S["yt_ps"], at("yt_ps", l) + n - 1)
                    own.link(TT(ysum[n % 2], PS[:, 1, :], ycross, ALU.add))
                    own.link(RED(st8[:, 0, :], y8(n), AX.X, ALU.add))
                    own.link(TS(st8[:, 1, :], st8[:, 0, :], 1.0 / 64, None, ALU.mult))
                    TT(y8(n), y8(n), b8(st8[:, 1, :]), ALU.subtract).then_inc(S["y_mid"], 1)

                def variance(n):
                    dve.wait_ge(S["y_sq"], at("y_sq", l) + n + 1)
                    own.link(RED(st8[:, 2, :], s8, AX.X, ALU.add))
                    TS(st8[:, 3, :], st8[:, 2, :], 1.0 / 64, 1e-6, ALU.mult, ALU.add).then_inc(S["y_var"], 1)

                def normalise(n):
                    dve.wait_ge(S["y_pow"], at("y_pow", l) + n + 1)
                    TT(y8(n), y8(n), b8(st8[:, 2, :]), ALU.mult).then_inc(S["y_norm"], 1)

                def gated(n):
                    tok = slice((n + tq) * P, (n + tq + 1) * P)
                    dve.wait_ge(S["yt_ps"], at("yt_ps", l) + n + 1)
                    gates = R[:, G + 6:G + 10, tok]
                    own.link(TT(gates, PS[:, 3, :].rearrange("p (j t) -> p j t", j=4), gates, ALU.mult))
                    TT(gates[:, 0:2, :], gates[:, 0:2, :], gates[:, 2:4, :], ALU.add).then_inc(S["yb_sum"], 1)

                def gated_lo(n):
                    t = n + tq
                    dve.wait_ge(S["yb_hi"], at("yb_hi", l) + n + 1)
                    STT(hlr(Y + 2, 2, 1, t * P, P), R[:, G + 6:G + 8, t * P:(t + 1) * P], XS * 0.5 * UNS,
                        hlr(Y + 2, 2, 0, t * P, P), ALU.mult, ALU.subtract).then_inc(S["yb_done"], 1)

                dve.wait_ge(S["kv_fwd"], at("kv_fwd", l) + NTILE - 1)
                dve.wait_ge(S["kv_ps"], at("kv_ps", l) + NTILE)
                for t in range(1, tq + 1):
                    forward_state(t)
                dve.wait_ge(S["d_tab"], at("d_tab", l) + 16)
                for n in range(NQ + 2):
                    if n < NQ:
                        masks(n)
                    if n >= 2:
                        gated(n - 2)
                    if 1 <= n <= NQ:
                        variance(n - 1)
                    if n + tq + 1 < NTILE:
                        forward_state(n + tq + 1)
                    if n >= 2:
                        gated_lo(n - 2)
                    if n < NQ:
                        centre(n)
                    if 1 <= n <= NQ:
                        normalise(n - 1)

                dve.wait_ge(S["a_tab"], at("a_tab", l) + 64)
                for v in range(A_UNITS):
                    lo_part(u0 + 16 + v + 1, (v + 1) % 2, KD)
                    for m, (i, c0, c1) in enumerate(rotary(l)):
                        if i != v - 1:
                            continue
                        w, row = c1 - c0, arow(i)
                        dve.wait_ge(S["perm_ps"], at("perm_ps", l) + m + 1)
                        TT(T[:, 0:w], PS[:, 6 + m % 2, 0:w], xrow(3)[:, c0:c1], ALU.mult)
                        own.link(TT(row[:, c0:c1], row[:, c0:c1], xrow(2)[:, c0:c1], ALU.mult))
                        if m:
                            dve.wait_ge(S["rot_lo"], at("rot_lo", l) + m)
                        TT(T[:, 512:512 + w], row[:, c0:c1], T[:, 0:w], ALU.add).then_inc(S["rot"], 1)
                        dve.wait_ge(S["rot_hi"], at("rot_hi", l) + m + 1)
                        TT(arow16(i, c0 + c1, 2 * c1), T[:, 512:512 + w], arow16(i, 2 * c0, c0 + c1),
                           ALU.subtract).then_inc(S["rot_lo"], 1)
                for n, (m, i, j, c0, c1) in enumerate(stacks(l)):
                    if n % 2:
                        dve.wait_ge(S["stk_ps"], at("stk_ps", l) + n + 1)
                        nc.vector.tensor_copy((Kst, Qst)[i // 2][:, 4 * (i % 2) + j, c0:c1],
                                              PS[:, STACK_BANKS[n % 4], 0:c1 - c0]).then_inc(S["stk_dve"], 1)
                for t in range(NTILE):
                    dve.wait_ge(S["vt_hi"], at("vt_hi", l) + t + 1)
                    TT(Vst[:, t, :, 1, :], PS[:, VALUE_BANKS[t % 4], 0:256].rearrange("p (h e) -> p h e", h=HA),
                       Vst[:, t, :, 0, :], ALU.subtract).then_inc(S["vt_done"], 1)
                for run, t_first, nt, nk in attend_runs(l):
                    attend(l, run, t_first, nt, nk)
                modulation(2 * l + 1, ada0(l), ADA_PER[l] * (LAT // P), ADA_COL)
                dve.wait_ge(S["vec_ready"], 2 * l + 2)

                units(unit0(l, "out"), KD, lambda i, j, r: None)
                inverse_root(4 * l + 1, t0)
                add_to_h(l, 0, U, t0)
                inverse_root(4 * l + 2, t0)
                scale_rows(l, 1, t0)

                done = 0
                for q, nf in enumerate(FPARTS):
                    def ffn_evac(i, j, r):
                        if j == 0:
                            dve.wait_ge(S["g_tanh"], at("g_tanh", l) + r + (done + 1))
                            STT(xrow(2)[:, t0:], xrow(1)[:, t0:], 1.0, slot(0, t0), ALU.add, ALU.mult).then_inc(S["slot_free"], 1)
                        else:
                            dve.wait_ge(S["units"], i + (unit0(l, "gu", q) + 1))
                            dve.wait_ge(S["slot_free"], i + unit0(l, "gu", q))
                            STT(xrow(3)[:, t0:], xrow(2)[:, t0:], 2.0 ** -17, slot(1, t0), ALU.mult, ALU.mult).then_inc(S["slot_free"], 1)
                            dve.wait_ge(S["ffn_hi"], at("ffn_hi", l) + r + (done + 1))
                            TT(R16[:, bass.ds(G + r, 1), TOK + t0:2 * TOK], xrow(3)[:, t0:].rearrange("p (a t) -> p a t", a=1),
                               R16[:, bass.ds(G + r, 1), t0:TOK], ALU.subtract).then_inc(S["ffn_lo"], 1)

                    def down_evac(i, j, r):
                        if q:
                            dve.wait_ge(S["units"], i + (unit0(l, "down", q) + 1))
                            row = R[:, bass.ds(Y + i, 1), t0:]
                            STT(row, slot(j, t0).rearrange("p (a t) -> p a t", a=1), UNS, row,
                                ALU.mult, ALU.add).then_inc(S["slot_free"], 1)

                    units(unit0(l, "gu", q), 2 * nf, ffn_evac)
                    units(unit0(l, "down", q), KD, down_evac)
                    done += nf
                if l == 0:
                    modulation(2, ADA_F0, ADA_FFN, 3072)
                    dve.wait_ge(S["vec_ready"], 3)
                inverse_root(4 * l + 3, t0)
                add_to_h(l, 1, Y, t0)
                if l < LAYERS - 1:
                    inverse_root(4 * l + 4, t0)

        @block.gpsimd
        def _(pool):
            TT = nc.gpsimd.tensor_tensor
            own = Chain(pool, S["pool_own"])

            def add_squares(inst, t0):
                for d in range(KD):
                    q = KD * inst + d
                    pool.wait_ge(S["sq_ready"], q + 1)
                    if d == 0:
                        if inst:
                            pool.wait_ge(S["sumsq"], inst)
                        nc.gpsimd.tensor_copy(xrow(0)[:, t0:], xrow(2)[:, t0:]).then_inc(S["sq_used"], 1)
                    else:
                        pool.wait_ge(S["sq_used"], q)
                        TT(xrow(0)[:, t0:], xrow(0)[:, t0:], xrow(2 + d % 2)[:, t0:], ALU.add).then_inc(S["sq_used"], 1)

            pool.memset(nhalf[:, :], -0.5).then_inc(S["small_const"], 1)
            pool.memset(epsv[:, 0:1], 1e-6).then_inc(S["small_const"], 1)
            pool.memset(epsv[:, 1:2], 1e-5).then_inc(S["small_const"], 1)
            pool.memset(beta[:, :], 0.0)
            add_squares(0, 0)

            for l in range(LAYERS):
                t0 = first_tok(l)
                u0 = unit0(l, "in")
                pool.wait_ge(S["u_done"], 2 * KD * l + KD)
                if l:
                    pool.wait_ge(S["slot_free"], u0)
                gaps = [(0, HALF), (HALF + CTX, HALF), (PADW - HALF, HALF)] if not t0 else \
                    [(0, 2 * HALF + CTX), (PADW - HALF, HALF)]
                for g0, n in gaps:
                    pool.memset(Gpad[:, 2:4, g0:g0 + n], 0.0)
                    last = pool.memset(Xpad[:, 0:2, g0:g0 + n], 0.0)
                last.then_inc(S["pads_zero"], 1)
                pool.wait_ge(S["pads_zero"], at("pads_zero", l) + 1)
                pool.wait_ge(S["cd_tab"], at("cd_tab", l) + 64)
                for j in range(2):
                    pool.wait_ge(S["slot_free"], u0 + 1 + j)
                    src = Gpad[:, 2 + j, :]
                    a_, b_ = Gpad[:, 4, :], Gpad[:, 5, :]
                    own.link(TT(a_[:, 1:PADW], src[:, 0:PADW - 1], src[:, 1:PADW], ALU.add))
                    own.link(TT(b_[:, 2:PADW - 1], a_[:, 1:PADW - 2], a_[:, 3:PADW], ALU.add))
                    if j:
                        own.link(TT(a_[:, 4:PADW - 3], b_[:, 2:PADW - 5], b_[:, 6:PADW - 1], ALU.add))
                        own.link(TT(b_[:, 8:PADW - 7], a_[:, 4:PADW - 11], a_[:, 12:PADW - 3], ALU.add))
                    for half, w in ((0, a_), (64, b_)):
                        for p0, c0, n in segs(l):
                            last = TT(R[half:half + 64, Y + 2 + j, c0:c0 + n], w[half:half + 64, p0:p0 + n],
                                      R[half:half + 64, Y + j, c0:c0 + n], ALU.mult)
                    own.link(last)
                    for p0, c0, n in segs(l):
                        last = TT(R[:, Y + 2 + j, c0:c0 + n], R[:, Y + 2 + j, c0:c0 + n], src[:, p0:p0 + n], ALU.subtract)
                    last.then_inc(S["pooled"], 1)
                    pool.wait_ge(S["pooled"], at("pooled", l) + j + 1)
                pool.wait_ge(S["roped"], at("roped", l) + 4)
                pool.memset(Sf[:, 0, :], 0.0)
                pool.memset(Sb[:, B_ORDER[0], :], 0.0).then_inc(S["states_zero"], 1)
                for n in range(NTILE - t0 // P):
                    pool.wait_ge(S["y_var"], at("y_var", l) + n + 1)
                    TT(st8[:, 2, :], st8[:, 3, :], nhalf[:, 0:1].to_broadcast([P, 8]), ALU.pow).then_inc(S["y_pow"], 1)
                for run, t_first, nt, nk in attend_runs(l):
                    with pool.Fori(0, nt) as r:
                        pool.wait_ge(S[f"o_var_{run}{l}"], r + 1)
                        TT(st8[:, 2, 0:4], st8[:, 1, 0:4], nhalf[:, 0:1].to_broadcast([P, 4]),
                           ALU.pow).then_inc(S[f"o_pow_{run}{l}"], 1)
                for inst in range(4 * l + 1, 4 * l + (5 if l < LAYERS - 1 else 4)):
                    add_squares(inst, t0)



def _tables():
    f = np.float32
    tok = np.arange(LAT)
    row, col = (tok // 64).astype(f), (tok % 64).astype(f)

    def rope(d):
        nf = d // 4
        inv = (f(10000.0) ** (-np.arange(nf, dtype=f) / f(nf))).astype(f)
        ang = np.concatenate([row[:, None] * inv, col[:, None] * inv], axis=-1).astype(f)
        c, s = np.cos(ang).T.astype(f), np.sin(ang).T.astype(f)
        C, Sn = np.ones((P, TOK), f), np.zeros((P, TOK), f)
        C[:, CTX:] = np.tile(np.concatenate([c, c]), (P // d, 1))
        Sn[:, CTX:] = np.tile(np.concatenate([-s, s]), (P // d, 1))
        perm = np.zeros((P, P), f)
        for m in range(P):
            perm[m - m % d + (m % d + d // 2) % d, m] = 1
        return np.stack([C, Sn]), perm

    ropeA, permA = rope(DQ)
    ropeB, permB = rope(DK)
    stk = np.zeros((P, 4, 352), np.float16)
    for j in range(4):
        for b in (0, 1, 4, 5, 6, 8, 10):
            for d in range(32):
                stk[32 * j + d, j, 32 * b + d] = 1
    gam = np.exp(np.array(LOG_GAMMA))
    i = np.arange(P)
    dist = i[None, :] - i[:, None]
    dmask = np.zeros((P, 2, HB, P))
    rtab = np.zeros((P, 18))
    for h in range(HB):
        pw = gam[h] ** np.abs(dist) * DK ** -0.5
        dmask[:, 0, h] = np.where(dist >= 0, pw, 0)
        dmask[:, 1, h] = np.where(dist <= 0, pw, 0)
        rtab[:, h] = gam[h] ** (i + 1)
        rtab[:, 4 + h] = gam[h] ** (P - i)
        rtab[:, 8 + h] = gam[h] ** (P - 1 - i) * DK ** -0.5
        rtab[:, 12 + h] = gam[h] ** i * DK ** -0.5
        rtab[64 * (h % 2):64 * (h % 2) + 64, 16 + h // 2] = gam[h] ** P
    cnt = np.zeros((2, P, TOK))
    for g, w in enumerate((2, 4, 8, 16)):
        for n, c0 in ((CTX, 0), (LAT, CTX)):
            pos = np.arange(n)
            k = np.clip(pos + w - w // 2, 0, n) - np.clip(pos - w // 2, 0, n)
            cnt[g // 2, 64 * (g % 2):64 * (g % 2) + 64, c0:c0 + n] = 1.0 / k
    return {"ident": np.eye(P, dtype=f), "ones": np.ones((P, P), f), "rtab": rtab.astype(f),
            "ropeA": ropeA, "ropeB": ropeB, "permA": permA, "permB": permB, "stk": stk.reshape(P, -1).view(f),
            "dmask": dmask.astype(f).reshape(P, -1), "cnt": cnt.astype(f)}


def _units(w, order=None):
    L, k, n = w.shape
    u = w.reshape(L, k // P, P, n // P, P).transpose(0, 3, 2, 1, 4)
    return np.ascontiguousarray(u if order is None else u[:, order])


def _cols(v):
    return v.reshape(v.shape[0], -1, P).transpose(2, 0, 1)


def layout(i):
    L = LAYERS
    arr = _tables()
    tokens = np.concatenate([i["ctx"][0], i["x"][0]])
    arr["x"] = np.ascontiguousarray(tokens.T.reshape(KD, P, TOK))
    arr["c2"] = np.ascontiguousarray(np.stack([i["c"][0], i["c_ctx"]], -1).reshape(KD, P, 2).transpose(1, 0, 2))
    lam = np.stack([i["lam_q1"], i["lam_k1"], i["lam_q2"], i["lam_k2"]], 1).reshape(1, -1)
    arr["lam"] = np.ascontiguousarray(np.broadcast_to(lam, (P, lam.size)))
    arr["w_ada"] = _units(i["w_ada"]).reshape(L * 48, P, KD, P)
    arr["w_in"] = _units(i["w_in"], [16, 17, 20, 21, 18, 19, 4, 5, 6, 7, 10, 11, 12, 13, 14, 15, 0, 1, 8, 9, 2, 3])
    arr["w_out"] = _units(i["w_out"])
    g, u = _units(i["w_ffn_gate"]), _units(i["w_ffn_up"])
    arr["w_gu"] = np.ascontiguousarray(np.stack([g, u], 2).reshape(L, 2 * NF, P, KD, P))
    f0 = 0
    for q, nf in enumerate(FPARTS):
        arr[f"w_down{q}"] = _units(i["w_ffn_down"][:, f0 * P:(f0 + nf) * P])
        f0 += nf
    pw = i["w_conv_out"].reshape(L, 2, P, 256).transpose(0, 2, 1, 3).reshape(L, P, 512)
    wp = np.zeros((L, P, 2, P), np.float32)
    for gi in range(4):
        o = 64 * (gi % 2)
        wp[:, o:o + 64, gi // 2, o:o + 64] = i["w_pool"][:, gi]
    arr["swb"] = np.ascontiguousarray(np.concatenate([pw, wp.reshape(L, P, 256)], -1))
    sub = np.broadcast_to(i["g_subln"][:, None, :], (L, 2, DV)).reshape(L, P)
    cw = i["conv_w"][:, :, 0, :].reshape(L, TAPS, 2, P).transpose(3, 0, 2, 1).reshape(P, L, 2 * TAPS)
    parts = [np.concatenate([_cols(i["g_pre_mix"]), _cols(i["g_pre_ffn"])], -1),
             np.concatenate([_cols(i["g_post_mix"]), _cols(i["g_post_ffn"])], -1),
             cw, _cols(i["conv_b"]), _cols(i["conv_ln_g"]), _cols(i["conv_ln_b"]), _cols(i["s_pool"]), _cols(sub)]
    arr["b_ada"] = np.ascontiguousarray(_cols(i["b_ada"]).reshape(P, -1))
    arr["small"] = np.ascontiguousarray(np.concatenate(parts, -1))
    return arr


def kernel(**inputs):
    import concourse.bacc as _bacc
    from concourse.bass_utils import run_bass_kernel_spmd as _run

    arrays = layout({k: np.asarray(v) for k, v in inputs.items()})
    nc = _bacc.Bacc("TRN2", target_bir_lowering=False, num_devices=1)
    aps = {k: nc.dram_tensor("in_" + k, v.shape, mybir.dt.from_np(v.dtype), kind="ExternalInput").ap() for k, v in arrays.items()}
    out = nc.dram_tensor("out", (KD, P, LAT), F32, kind="ExternalOutput").ap()
    build(nc, aps, out)
    r = _run(nc, [{"in_" + k: v for k, v in arrays.items()}], core_ids=[0])
    got = r.results[0]["out"]
    return np.ascontiguousarray(got.reshape(1, D, LAT).transpose(0, 2, 1))
```
